# Optimizing a Trainium2 kernel written in Bass

```python
import jax, jax.numpy as jnp
from jax import lax
import numpy as np

D_MODEL = 1024
BATCH = 1
SEQ = 256
DEPTH = 1

CHUNK = 64
Q_BLOCK = 128
RET_HEADS = 4
RET_HEAD_DIM = 128
RET_WIDTH = RET_HEADS * RET_HEAD_DIM
FOX_HEADS = 8
FOX_HEAD_DIM = 64
FOX_WIDTH = FOX_HEADS * FOX_HEAD_DIM
MIX_WIDTH = RET_WIDTH + FOX_WIDTH
IN_PROJ_WIDTH = 4 * RET_WIDTH + 3 * FOX_WIDTH + FOX_HEADS
ROPE_BASE = 10000.0
N_EXPERTS = 32
TOP_K = 4
D_FF = D_MODEL
SWIGLU_ALPHA = 1.702
SWIGLU_LIMIT = 7.0
EXPERT_BLOCK = 256
RMS_EPS = 1e-5
GN_EPS = 1e-5

kernel_name = "hybrid_retention_fox_moe_block"

def rms_norm(x, g):
    xf = x.astype(jnp.float32)
    y = xf * lax.rsqrt(jnp.mean(xf * xf, axis=-1, keepdims=True) + RMS_EPS)
    return (y * g.astype(jnp.float32)).astype(x.dtype)

def rotary(x, pos):
    half = x.shape[-1] // 2
    inv_freq = ROPE_BASE ** (-jnp.arange(half, dtype=jnp.float32) / half)
    ang = pos[:, None] * inv_freq[None, :]
    cos = jnp.cos(ang)[None, :, None, :]
    sin = jnp.sin(ang)[None, :, None, :]
    x1, x2 = x[..., :half], x[..., half:]
    return jnp.concatenate([x1 * cos - x2 * sin, x1 * sin + x2 * cos], axis=-1)

def retention(q, k, v, g):
    dtype = q.dtype
    B, S, H, d = q.shape
    NC = S // CHUNK
    log_gamma = jnp.log1p(-jnp.exp2(-5.0 - jnp.arange(H, dtype=jnp.float32)))
    qf = q.astype(jnp.float32).reshape(B, NC, CHUNK, H, d)
    kf = (k.astype(jnp.float32) * (d ** -0.5)).reshape(B, NC, CHUNK, H, d)
    vf = v.astype(jnp.float32).reshape(B, NC, CHUNK, H, d)
    pos_c = jnp.arange(CHUNK, dtype=jnp.float32)
    dist = jnp.abs(pos_c[:, None] - pos_c[None, :])
    decay_intra = jnp.exp(log_gamma[:, None, None] * dist)
    scores = jnp.einsum('bnqhd,bnkhd->bnhqk', qf, kf) * decay_intra
    o_intra = jnp.einsum('bnhqk,bnkhe->bnqhe', scores, vf)
    q_w = jnp.exp(log_gamma[None, :] * (pos_c[:, None] + 1.0))
    k_w = jnp.exp(log_gamma[None, :] * (CHUNK - 1.0 - pos_c[:, None]))
    chunk_decay = jnp.exp(log_gamma * CHUNK)[None, :, None, None]
    q_t = jnp.moveaxis(qf * q_w[:, :, None], 1, 0)
    k_t = jnp.moveaxis(kf * k_w[:, :, None], 1, 0)
    v_t = jnp.moveaxis(vf, 1, 0)

    def step(state, inp):
        qc, kc, vc = inp
        o = jnp.einsum('bqhd,bhde->bqhe', qc, state)
        new_state = state * chunk_decay + jnp.einsum('bkhd,bkhe->bhde', kc, vc)
        return new_state, o

    state0 = jnp.zeros((B, H, d, d), jnp.float32)
    _, o_inter = lax.scan(step, state0, (q_t, k_t, v_t))
    o = (o_intra + jnp.moveaxis(o_inter, 0, 1)).reshape(B, S, H, d)
    mu = jnp.mean(o, axis=-1, keepdims=True)
    var = jnp.mean(jnp.square(o - mu), axis=-1, keepdims=True)
    o = (o - mu) * lax.rsqrt(var + GN_EPS)
    o = o * jax.nn.silu(g.astype(jnp.float32))
    return o.reshape(B, S, H * d).astype(dtype)

def forgetting_attention(q, k, v, z_f, b_f):
    dtype = q.dtype
    B, S, H, d = q.shape
    NQB = S // Q_BLOCK
    log_f = jax.nn.log_sigmoid(z_f.astype(jnp.float32) + b_f.astype(jnp.float32))
    F = jnp.cumsum(log_f, axis=1).transpose(0, 2, 1)
    qh = q.astype(jnp.float32).transpose(0, 2, 1, 3) * (d ** -0.5)
    kh = k.astype(jnp.float32).transpose(0, 2, 1, 3)
    vh = v.astype(jnp.float32).transpose(0, 2, 1, 3)
    q_blocks = qh.reshape(B, H, NQB, Q_BLOCK, d).transpose(2, 0, 1, 3, 4)
    F_blocks = F.reshape(B, H, NQB, Q_BLOCK).transpose(2, 0, 1, 3)
    t_blocks = jnp.arange(S, dtype=jnp.int32).reshape(NQB, Q_BLOCK)
    s_idx = jnp.arange(S, dtype=jnp.int32)

    def block(args):
        q_i, F_i, t_i = args
        logits = jnp.einsum('bhqd,bhkd->bhqk', q_i, kh) + F_i[..., None] - F[:, :, None, :]
        mask = s_idx[None, :] <= t_i[:, None]
        logits = jnp.where(mask[None, None], logits, -jnp.inf)
        p = jax.nn.softmax(logits, axis=-1)
        return jnp.einsum('bhqk,bhkd->bhqd', p, vh)

    out = lax.map(block, (q_blocks, F_blocks, t_blocks))
    out = out.transpose(1, 0, 3, 2, 4).reshape(B, S, H * d)
    return out.astype(dtype)

def clamped_swiglu(h):
    x_glu, x_lin = h[..., :D_FF], h[..., D_FF:]
    x_glu = jnp.minimum(x_glu, SWIGLU_LIMIT)
    x_lin = jnp.clip(x_lin, -SWIGLU_LIMIT, SWIGLU_LIMIT)
    return x_glu * jax.nn.sigmoid(SWIGLU_ALPHA * x_glu) * (x_lin + 1.0)

def moe(x, w_router, b_router, w1, b1, w2, b2):
    B, S, D = x.shape
    T = B * S
    A = T * TOP_K
    xs = x.reshape(T, D)
    logits = xs.astype(jnp.float32) @ w_router.astype(jnp.float32) + b_router.astype(jnp.float32)
    top_val, top_idx = lax.top_k(logits, TOP_K)
    gates = jax.nn.softmax(top_val, axis=-1)
    e_flat = top_idx.reshape(A).astype(jnp.int32)
    tok_flat = jnp.repeat(jnp.arange(T, dtype=jnp.int32), TOP_K)
    gate_flat = gates.reshape(A)
    order = jnp.argsort(e_flat, stable=True)
    e_s, tok_s, gate_s = e_flat[order], tok_flat[order], gate_flat[order]
    counts = jax.ops.segment_sum(jnp.ones((A,), jnp.int32), e_flat, num_segments=N_EXPERTS)
    starts = jnp.cumsum(counts) - counts
    padded = (counts + EXPERT_BLOCK - 1) // EXPERT_BLOCK * EXPERT_BLOCK
    pad_ends = jnp.cumsum(padded)
    pad_starts = pad_ends - padded
    dest = pad_starts[e_s] + (jnp.arange(A, dtype=jnp.int32) - starts[e_s])
    NB = (A + EXPERT_BLOCK - 1) // EXPERT_BLOCK + N_EXPERTS
    buf_tok = jnp.full((NB * EXPERT_BLOCK,), T, jnp.int32).at[dest].set(tok_s)
    buf_gate = jnp.zeros((NB * EXPERT_BLOCK,), jnp.float32).at[dest].set(gate_s)
    block_start = jnp.arange(NB, dtype=jnp.int32) * EXPERT_BLOCK
    block_exp = jnp.minimum(jnp.searchsorted(pad_ends, block_start, side='right'),
                            N_EXPERTS - 1).astype(jnp.int32)
    x_pad = jnp.concatenate([xs, jnp.zeros((1, D), xs.dtype)], axis=0)

    def expert_block(args):
        tok_b, gate_b, e = args
        xb = x_pad[tok_b]
        h = xb @ w1[e] + b1[e]
        y = clamped_swiglu(h) @ w2[e] + b2[e]
        return y * gate_b[:, None].astype(y.dtype)

    y_blocks = lax.map(expert_block, (buf_tok.reshape(NB, EXPERT_BLOCK),
                                      buf_gate.reshape(NB, EXPERT_BLOCK), block_exp))
    out = jnp.zeros((T + 1, D), y_blocks.dtype).at[buf_tok].add(y_blocks.reshape(-1, D))
    return out[:T].reshape(B, S, D).astype(x.dtype)

def setup_inputs(seed: int = 0) -> dict:
    key = jax.random.key(seed)
    ks = jax.random.split(key, 14)
    f32 = jnp.float32
    x = jax.random.normal(ks[0], (BATCH, SEQ, D_MODEL), f32)
    norm_mix_g = 1.0 + 0.02 * jax.random.normal(ks[1], (DEPTH, D_MODEL), f32)
    w_in = jax.random.normal(ks[2], (DEPTH, D_MODEL, IN_PROJ_WIDTH), f32) * D_MODEL ** -0.5
    b_forget = jax.random.uniform(ks[3], (DEPTH, FOX_HEADS), f32, minval=1.0, maxval=6.0)
    w_out = jax.random.normal(ks[4], (DEPTH, MIX_WIDTH, D_MODEL), f32) * MIX_WIDTH ** -0.5
    norm_ffn_g = 1.0 + 0.02 * jax.random.normal(ks[5], (DEPTH, D_MODEL), f32)
    w_router = jax.random.normal(ks[6], (DEPTH, D_MODEL, N_EXPERTS), f32) * D_MODEL ** -0.5
    b_router = 0.01 * jax.random.normal(ks[7], (DEPTH, N_EXPERTS), f32)
    w_exp_in = jax.random.normal(ks[8], (DEPTH, N_EXPERTS, D_MODEL, 2 * D_FF), f32) * D_MODEL ** -0.5
    b_exp_in = 0.01 * jax.random.normal(ks[9], (DEPTH, N_EXPERTS, 2 * D_FF), f32)
    w_exp_out = jax.random.normal(ks[10], (DEPTH, N_EXPERTS, D_FF, D_MODEL), f32) * D_FF ** -0.5
    b_exp_out = 0.01 * jax.random.normal(ks[11], (DEPTH, N_EXPERTS, D_MODEL), f32)
    norm_final_g = 1.0 + 0.02 * jax.random.normal(ks[12], (D_MODEL,), f32)
    return {"x": x, "norm_mix_g": norm_mix_g, "w_in": w_in, "b_forget": b_forget,
            "w_out": w_out, "norm_ffn_g": norm_ffn_g, "w_router": w_router,
            "b_router": b_router, "w_exp_in": w_exp_in, "b_exp_in": b_exp_in,
            "w_exp_out": w_exp_out, "b_exp_out": b_exp_out, "norm_final_g": norm_final_g}

def reference(x, norm_mix_g, w_in, b_forget, w_out, norm_ffn_g, w_router, b_router,
              w_exp_in, b_exp_in, w_exp_out, b_exp_out, norm_final_g):
    B, S, _ = x.shape
    pos = jnp.arange(S, dtype=jnp.float32)
    split_points = [RET_WIDTH * i for i in range(1, 5)] + \
                   [4 * RET_WIDTH + FOX_WIDTH * i for i in range(1, 4)]
    h = x
    for l in range(DEPTH):
        u = rms_norm(h, norm_mix_g[l])
        proj = u @ w_in[l]
        rq, rk, rv, rg, fq, fk, fv, fz = jnp.split(proj, split_points, axis=-1)
        rh = lambda t: t.reshape(B, S, RET_HEADS, RET_HEAD_DIM)
        fh = lambda t: t.reshape(B, S, FOX_HEADS, FOX_HEAD_DIM)
        o_ret = retention(rotary(rh(rq), pos), rotary(rh(rk), pos), rh(rv), rh(rg))
        o_fox = forgetting_attention(fh(fq), fh(fk), fh(fv), fz, b_forget[l])
        mix = jnp.concatenate([o_ret, o_fox], axis=-1)
        h = h + mix @ w_out[l]
        h = h + moe(rms_norm(h, norm_ffn_g[l]), w_router[l], b_router[l],
                    w_exp_in[l], b_exp_in[l], w_exp_out[l], b_exp_out[l])
    return rms_norm(h, norm_final_g)


_drawn_inputs = setup_inputs


def setup_inputs(seed=0):
    import zlib

    import numpy as np

    out = dict(_drawn_inputs(seed))
    spreads = {}
    factors = {'b_exp_in': 8.0, 'b_exp_out': 8.0, 'norm_final_g': 2.886}
    for name, (base, spread) in spreads.items():
        noise = np.random.default_rng([zlib.crc32(name.encode()), seed]).standard_normal(out[name].shape)
        drawn = base * np.exp(spread * noise) if base else spread * noise
        out[name] = __import__('jax').numpy.asarray(drawn.astype(out[name].dtype))
    for name, factor in factors.items():
        out[name] = (out[name] * factor).astype(out[name].dtype)
    return out
```

```python
from contextlib import ExitStack

import numpy as np

import concourse.bass as bass
from concourse import mybir

F32 = mybir.dt.float32
BF16 = mybir.dt.bfloat16
I32 = mybir.dt.int32
U32 = mybir.dt.uint32
ALU = mybir.AluOpType
ACT = mybir.ActivationFunctionType
AX = mybir.AxisListType

P = 128
SEQ, DM = 256, 1024
TT = SEQ // P
KC = DM // P
NW = 512
RET_HEADS, RET_D = 4, 128
FOX_HEADS, FOX_D = 8, 64
CHUNK = 64
EXPERTS, TOP_K = 32, 4
SLOTS = 64
ROUNDS = SEQ // SLOTS
UNPICKED = 1024.0
RMS_EPS = GN_EPS = 1e-5
LIMIT, ALPHA = 7.0, 1.702
MASKED = -1e30

CONST_COLS = [("ident", P), ("before", P), ("ones", P), ("causal", P), ("cos", TT * 64),
              ("sin", TT * 64), ("negsin", TT * 64), ("decay", RET_HEADS * 384),
              ("slot_ids", 4 * SLOTS), ("expert_ids", EXPERTS), ("piece_row", EXPERTS + 2)]
CONST_AT = {}
_n = 0
for _name, _w in CONST_COLS:
    CONST_AT[_name] = (_n, _w)
    _n += _w
CONST_W = _n


def constant_table():
    t = np.zeros((P, CONST_W), np.float32)

    def put(name, a):
        at, w = CONST_AT[name]
        t[:a.shape[0], at:at + w] = a.reshape(a.shape[0], w)

    i = np.arange(P)
    put("ident", np.eye(P, dtype=np.float32))
    put("before", (i[:, None] < i[None, :]).astype(np.float32))
    put("ones", np.ones((P, P), np.float32))
    put("causal", np.where(i[None, :] <= i[:, None], 0.0, MASKED).astype(np.float32))
    half = RET_D // 2
    freq = np.float32(10000.0) ** (-np.arange(half, dtype=np.float32) / np.float32(half))
    angle = (np.arange(SEQ, dtype=np.float32)[:, None] * freq[None, :]).reshape(TT, P, half)
    angle = angle.transpose(1, 0, 2).astype(np.float64)
    put("cos", np.cos(angle).astype(np.float32))
    put("sin", np.sin(angle).astype(np.float32))
    put("negsin", -np.sin(angle).astype(np.float32))
    log_gamma = np.log1p(-np.exp2(-5.0 - np.arange(RET_HEADS)))
    dec = np.zeros((P, RET_HEADS, 384))
    for key0, query0, at, n in ((0, 0, 0, SEQ), (P, P, SEQ, P)):
        s = key0 + i[:, None]
        q = query0 + np.arange(n)[None, :]
        seen = s // CHUNK <= q // CHUNK
        for h in range(RET_HEADS):
            dec[:, h, at:at + n] = np.where(seen, np.exp(log_gamma[h] * np.abs(q - s)), 0.0)
    put("decay", (dec * RET_D ** -0.5).astype(np.float32))
    ids = np.arange(SLOTS)
    none = np.full(SLOTS, 0.5)
    put("slot_ids", np.broadcast_to(np.concatenate([ids, none, none, ids]), (P, 4 * SLOTS)).astype(np.float32))
    put("expert_ids", np.broadcast_to(np.arange(EXPERTS), (P, EXPERTS)).astype(np.float32))
    rows = np.zeros((P, EXPERTS + 2), np.float32)
    rows[:3 * EXPERTS, :EXPERTS] = np.tile(np.eye(EXPERTS), (3, 1))
    put("piece_row", rows)
    return t


GROUPS = (
    [("uT0", "act"), ("uT1", "dve"), ("uT2", "act"), ("uT3", "dve")]
    + [("fq0", "act"), ("fq1", "act"), ("fz", "dve"), ("fk0", "act"), ("fk1", "act")]
    + [("fqT0", "dve"), ("fqT1", "dve")]
    + [("rq0", "dve"), ("rq1", "dve"), ("fkT0", "act"), ("fkT1", "act")]
    + [("rk0", "dve"), ("rk1", "dve")]
    + [(f"qk{g}", "act") for g in range(6)]
    + [("fv0", "act"), ("fv1", "act")]
    + [("rqT0", "dve"), ("rqT1", "dve"), ("rkT0", "act"), ("rkT1", "act")]
    + [("rv0", "act"), ("rv1", "act")]
    + [(f"pT{g}", "dve" if g % 2 else "act") for g in range(6)]
    + [(f"rs{h}", "dve") for h in range(RET_HEADS)]
    + [("rg0", "act"), ("rg1", "act"), ("pv0", "act"), ("pv1", "act")]
    + [("ro0", "dve"), ("ro1", "dve"), ("rT0", "act"), ("rT1", "act")]
    + [(f"out{g}", "dve") for g in range(4)]
    + [("vT0", "act"), ("vT1", "dve"), ("vT2", "act"), ("vT3", "dve")]
    + [("logits", "dve"), ("pos", "dve")]
)
GROUP_AT = {name: n for n, (name, _) in enumerate(GROUPS)}
BANKS = 8

QK_GROUPS = [(0, 0, 4, P), (0, 4, 4, P)] + [(1, 2 * j, 2, SEQ) for j in range(4)]
PT_GROUPS = [(0, 0, 0), (0, 0, 4), (1, 0, 0), (1, 0, 4), (1, 1, 0), (1, 1, 4)]

CHUNKS = [("fq", 2048, 0), ("fk", 2560, 1), ("rq", 0, 2), ("rk", 512, 3),
          ("fv", 3072, 0), ("rv", 1024, 1), ("rg", 1536, 2)]
FZ_COL = 3584
SLOT_OF = {name: s for name, _, s in CHUNKS}
OUT_ORDER = [4, 5, 6, 7, 0, 1, 2, 3]

ARENA = {
    "uT": (0, 2048), "xn": (2048, 2048), "fq": (4096, 1024), "p": (2048, 3072),
    "fk": (5120, 1024), "rq": (6144, 1024), "rk": (7168, 1024), "pT": (5120, 3072),
    "fqT": (8192, 1024), "fkTe": (9216, 1024), "fkTo": (10240, 1024),
    "fv": (11264, 1024), "zwork": (11264, 1792),
    "rqT": (12288, 1024), "rkT": (13312, 1024),
    "rv": (14336, 1024), "rg": (15360, 1024), "augq": (14336, 2048),
    "eg": (16384, 1024), "on": (17408, 1024), "augk": (16384, 2048),
    "rot": (18432, 1024), "rsc": (18432, 1536),
    "g_ffn": (0, 1024), "g_final": (1024, 1024),
    "bias": (8192, 3072), "bias_rest": (2048, 3072), "bias_rows": (11264, 1536), "bias_part": (12800, 1536),
    "u": (5120, 2048), "u_rest": (14336, 2048), "u_parts": (16384, 3072), "vT": (2048, 2048),
    "xT": (8192, 512), "gm": (8704, 512), "lc": (9216, 512), "lg": (9728, 512), "sg": (10240, 512),
    "act": (10752, 512), "actT": (4096, 512), "cab": (4608, 512), "gs": (7168, 512), "y": (7680, 512),
    "sq": (5120, 2048),
}
ARENA_W = 19968
ROOT_COLS = [slice(0, 2), slice(2, 6), slice(6, 10), slice(10, 11), slice(11, 12), slice(12, 14)]
RING_W2 = KC * 2 * DM
RING_W = RING_W2 + KC * DM


def build(nc, x, norm_mix_g, w_in, b_forget, w_out, norm_ffn_g, w_router, b_router,
          w_exp_in, b_exp_in, w_exp_out, b_exp_out, norm_final_g, table, out):
    with ExitStack() as ctx:
        def sb(name, shape, dt=F32):
            return ctx.enter_context(nc.sbuf_tensor(name, shape, dt))

        def sem(name):
            return ctx.enter_context(nc.semaphore(name))

        ring = sb("ring", [P, RING_W])
        arena = sb("arena", [P, ARENA_W])
        const = sb("const", [P, CONST_W])
        acc = sb("acc", [P, TT, DM])
        mixT = sb("mixT", [P, KC, SEQ])
        w_z = sb("w_z", [P, KC, FOX_HEADS])
        g_mix = sb("g_mix", [P, KC])
        b_fox = sb("b_fox", [FOX_HEADS, 1])
        w_rt = sb("w_rt", [P, KC, EXPERTS])
        b_rt = sb("b_rt", [P, EXPERTS])
        ss = sb("ss", [P, 2 * TT])
        negmax = sb("negmax", [P, TT * FOX_HEADS])
        psum_p = sb("psum_p", [P, TT * FOX_HEADS])
        rsum_p = sb("rsum_p", [P, TT * FOX_HEADS])
        stats = sb("stats", [P, RET_HEADS, 6])
        mv = sb("mv", [P, RET_HEADS, 2])
        root_of = sb("root_of", [P, 14])
        inv_root = sb("inv_root", [P, 14])
        root_t = sb("root_t", [P, 14])
        root_log = sb("root_log", [P, 14])
        logits = sb("logits", [P, TT, EXPERTS])
        top_v = sb("top_v", [P, TT, 8])
        top_i = sb("top_i", [P, TT, 8], U32)
        top_f = sb("top_f", [P, TT, TOP_K])
        gate4 = sb("gate4", [P, TT, TOP_K])
        gsum = sb("gsum", [P, TT])
        negtop = sb("negtop", [P, TT])
        picked = sb("picked", [P, TT, EXPERTS])
        onehot = sb("onehot", [P, EXPERTS])
        gates = sb("gates", [P, TT, EXPERTS])
        slot_of = sb("slot_of", [P, TT, EXPERTS + 2])
        most = sb("most", [1, 1], I32)
        sel = sb("sel", [P, TT, SLOTS], BF16)
        sel_row = sb("sel_row", [3 * EXPERTS, SLOTS], BF16)
        psum = ctx.enter_context(nc.psum_tensor("psum", [P, BANKS, NW], F32))

        def area(name, *shape):
            at, w = ARENA[name]
            v = arena[:, at:at + w]
            if len(shape) == 2:
                v = v.rearrange("p (a b) -> p a b", a=shape[0])
            if len(shape) == 3:
                v = v.rearrange("p (a b c) -> p a b c", a=shape[0], b=shape[1])
            return v

        def c(name):
            at, w = CONST_AT[name]
            return const[:, at:at + w]

        ident, before, ones, causal = c("ident"), c("before"), c("ones"), c("causal")
        cos, sin, negsin = (c(n).rearrange("p (t j) -> p t j", t=TT) for n in ("cos", "sin", "negsin"))
        decay = c("decay").rearrange("p (h j) -> p h j", h=RET_HEADS)
        slot_ids, expert_ids, piece_row = c("slot_ids"), c("expert_ids"), c("piece_row")

        uT = area("uT", KC, SEQ)
        xn = area("xn", TT, DM)
        fq, fk, fv = (area(n, TT, NW) for n in ("fq", "fk", "fv"))
        rq, rk, rv, rg, eg, on = (area(n, TT, NW) for n in ("rq", "rk", "rv", "rg", "eg", "on"))
        fqT, fkTe, fkTo = (area(n, 4, SEQ) for n in ("fqT", "fkTe", "fkTo"))
        rqT, rkT = (area(n, RET_HEADS, SEQ) for n in ("rqT", "rkT"))
        rot = area("rot", 2, NW)
        rsc = area("rsc", RET_HEADS, 384)
        augq, augk = (area(n, FOX_HEADS, SEQ) for n in ("augq", "augk"))
        zwork = area("zwork", 7, SEQ)
        p_w, pT_w = area("p"), area("pT")
        pT0 = pT_w[:, 0:2048].rearrange("p (h t) -> p h t", h=FOX_HEADS)
        pT1 = pT_w[:, 2048:3072].rearrange("p (h t) -> p h t", h=FOX_HEADS)
        vT = area("vT", KC, SEQ)
        u = area("u", TT, DM)
        u_rest = area("u_rest", TT, DM)
        u_parts = area("u_parts").bitcast(BF16).rearrange("p (s t d) -> p s t d", s=3, t=TT)
        bias, bias_rest = area("bias"), area("bias_rest")
        bias_rows, bias_part = area("bias_rows").bitcast(BF16), area("bias_part").bitcast(BF16)
        xT = area("xT", KC, SLOTS)
        gm, lc, lg, sg, act, y = (area(n) for n in ("gm", "lc", "lg", "sg", "act", "y"))
        actT, cab = area("actT", 4, P), area("cab", 4, P)
        gs = area("gs", TT, 4 * SLOTS)
        w1 = ring[:, 0:RING_W2].rearrange("p (k n) -> p k n", k=KC)
        w2 = ring[:, RING_W2:].rearrange("p (k n) -> p k n", k=KC)

        def chunk_ap(name):
            s = SLOT_OF[name]
            return ring[:, s * KC * NW:(s + 1) * KC * NW].rearrange("p (k n) -> p k n", k=KC)

        x_in, const_in, small_in = sem("x_in"), sem("const_in"), sem("small_in")
        chunk_in = {name: sem(f"{name}_in") for name, _, _ in CHUNKS}
        wout_in = [sem(f"wout_in{j}") for j in range(2)]
        bias_in, gains_in, aug_in = sem("bias_in"), sem("gains_in"), sem("aug_in")
        psum_full = sem("psum_full")
        freed = {"act": sem("freed_by_act"), "dve": sem("freed_by_dve")}
        dve_done, act_done = sem("dve_done"), sem("act_done")
        xn_ready, aug_zero, gate_f, neg_f = sem("xn_ready"), sem("aug_zero"), sem("gate_f"), sem("neg_f")
        z_abs, z_ln = sem("z_abs"), sem("z_ln")
        max_ready, p_ready, p_norm = sem("max_ready"), sem("p_ready"), sem("p_norm")
        fkz = sem("fkz")
        ron_ready, h_done, sq_done = sem("ron_ready"), sem("h_done"), sem("sq_done")
        u_ready, rows_ready, pool_done = sem("u_ready"), sem("rows_ready"), sem("pool_done")
        topv_ready, gexp_ready, picked_ready, routed = (
            sem("topv_ready"), sem("gexp_ready"), sem("picked_ready"), sem("routed"))
        w1_in = [sem(f"w1_in{k}") for k in range(KC)]
        w2_in = [sem(f"w2_in{k}") for k in range(KC)]
        w1_used, w2_used = sem("w1_used"), sem("w2_used")
        sel_ready, gath_done, xT_ready = sem("sel_ready"), sem("gath_done"), sem("xT_ready")
        row_ready, rows_used = sem("row_ready"), sem("rows_used")
        h_ready, gm_ready, lc_ready, lg_ready, sg_ready, a_ready = (
            sem("h_ready"), sem("gm_ready"), sem("lc_ready"), sem("lg_ready"), sem("sg_ready"), sem("a_ready"))
        aT_done, actT_ready, gs_ready, cT_done, cab_ready = (
            sem("aT_done"), sem("actT_ready"), sem("gs_ready"), sem("cT_done"), sem("cab_ready"))
        y_done, y_ready, comb_done, comb_added = sem("y_done"), sem("y_ready"), sem("comb_done"), sem("comb_added")
        root_ready, log_done, seed_ready = sem("root_ready"), sem("log_done"), sem("seed_ready")
        final_sq, final_ready, stored = sem("final_sq"), sem("final_ready"), sem("stored")

        x_dram = x[0].rearrange("(t p) d -> p t d", p=P)
        out_dram = out[0].rearrange("(t p) d -> p t d", p=P)
        w_in_dram = w_in[0].rearrange("(k p) n -> p k n", p=P)
        w_out_dram = w_out[0].rearrange("(k p) n -> p k n", p=P)

        def bank(name):
            return psum[:, GROUP_AT[name] % BANKS, :]

        def drained(name):
            n = GROUP_AT[name]
            return sum(1 for _, e in GROUPS[:n + 1] if e == GROUPS[n][1])

        def full(name):
            return GROUP_AT[name] + 1

        def free_bank(eng, name):
            n = GROUP_AT[name] - BANKS
            if n >= 0:
                before_name, reader = GROUPS[n]
                eng.wait_ge(freed[reader], drained(before_name))

        H0, H1, Y, XT, CT, AT, CB = 0, 1, 2, 3, 4, 5, 6

        block = ctx.enter_context(nc.Block())

        def rounds(eng, body):
            need = eng.alloc_register(f"need_{eng.engine.name}")
            eng.reg_mov(need, SLOTS)
            with eng.Fori(0, ROUNDS) as r:
                with eng.If(eng.snap(need) > r * SLOTS):
                    body(r)
                eng.wait_ge(routed, 1)
                eng.reg_load(need, most[0:1, 0:1])

        @block.sync
        def _(sp):
            def load_chunk(name):
                col = {n: cc for n, cc, _ in CHUNKS}[name]
                sp.dma_start(chunk_ap(name), w_in_dram[:, :, col:col + NW]).then_inc(chunk_in[name], 16)

            sp.dma_start(acc[:, :, :], x_dram).then_inc(x_in, 16)
            for name in ("fq", "fk", "rq", "rk"):
                load_chunk(name)
            for j in range(2):
                k0 = OUT_ORDER[4 * j]
                sp.dma_start(w2[:, 4 * j:4 * j + 4, :], w_out_dram[:, k0:k0 + 4, :]).then_inc(wout_in[j], 16)
            for name, gone in (("fv", "fq1"), ("rv", "fk1"), ("rg", "rq1")):
                sp.wait_ge(psum_full, full(gone))
                load_chunk(name)

            def one_round(r):
                with sp.Fori(0, EXPERTS) as e:
                    i = r * EXPERTS + e
                    for k in range(KC):
                        sp.wait_ge(w1_used, KC * i + k + 1)
                        sp.dma_start(w1[:, k, :], w_exp_in[0, e, k * P:(k + 1) * P, :]).then_inc(w1_in[k], 16)
                    for k in range(KC):
                        if k < KC - 1:
                            sp.wait_ge(w2_used, (KC - 1) * i + k + 1)
                        else:
                            sp.wait_ge(psum_full, full("out3"))
                            sp.wait_ge(y_done, i + 1)
                        sp.dma_start(w2[:, k, :], w_exp_out[0, e, k * P:(k + 1) * P, :]).then_inc(w2_in[k], 16)

            rounds(sp, one_round)
            sp.wait_ge(final_ready, 1)
            sp.dma_start(out_dram, acc[:, :, :]).then_inc(stored, 16)
            sp.wait_ge(stored, 16)

        @block.gpsimd
        def _(pool):
            nc.gpsimd.memset(augq[0:2, :, :], 1.0).then_inc(aug_zero, 1)
            nc.gpsimd.memset(augk[0:2, :, :], 1.0).then_inc(aug_zero, 1)
            pool.wait_ge(aug_zero, 2)
            pool.wait_ge(gate_f, 1)
            pool.dma_start(augq[1:2, :, :], zwork[0:FOX_HEADS, 5, :]).then_inc(aug_in, 16)
            pool.wait_ge(neg_f, 1)
            pool.dma_start(augk[0:1, :, :], zwork[0:FOX_HEADS, 6, :]).then_inc(aug_in, 16)
            pool.wait_ge(psum_full, full("qk5"))
            for s in range(3):
                rows = bias[s * EXPERTS:(s + 1) * EXPERTS, :]
                pool.dma_start(rows[:, 0:2 * DM], b_exp_in[0]).then_inc(bias_in, 16)
                pool.dma_start(rows[:, 2 * DM:3 * DM], b_exp_out[0]).then_inc(bias_in, 16)
            pool.wait_ge(psum_full, full("rg1"))
            pool.dma_start(area("g_ffn"), norm_ffn_g[0:1, :].to_broadcast([P, DM])).then_inc(gains_in, 16)
            pool.dma_start(area("g_final"), norm_final_g.rearrange("(a d) -> a d", a=1).to_broadcast([P, DM])) \
                .then_inc(gains_in, 16)
            n = 3 * EXPERTS
            pool.wait_ge(bias_in, 16 * 6)
            pool.wait_ge(psum_full, full("pv1"))
            nc.gpsimd.tensor_copy(bias_part[0:n, :], bias[0:n, :]).then_inc(pool_done, 1)
            pool.wait_ge(pool_done, 1)
            nc.gpsimd.tensor_tensor(bias_rest[0:n, :], bias[0:n, :], bias_part[0:n, :], ALU.subtract).then_inc(pool_done, 1)
            nc.gpsimd.tensor_copy(bias_rows[0:EXPERTS, :], bias_part[0:EXPERTS, :]).then_inc(pool_done, 1)
            pool.wait_ge(pool_done, 3)
            nc.gpsimd.tensor_copy(bias_part[0:n, :], bias_rest[0:n, :]).then_inc(pool_done, 1)
            pool.wait_ge(pool_done, 4)
            nc.gpsimd.tensor_copy(bias_rows[EXPERTS:2 * EXPERTS, :], bias_part[EXPERTS:2 * EXPERTS, :]).then_inc(rows_ready, 1)
            nc.gpsimd.tensor_tensor(bias_rows[2 * EXPERTS:n, :], bias_rest[2 * EXPERTS:n, :],
                                    bias_part[2 * EXPERTS:n, :], ALU.subtract).then_inc(rows_ready, 1)

        @block.tensor
        def _(pe):
            mm = nc.tensor.matmul
            for first in (cT_done, rows_used, y_done):
                pe.sem_inc(first, 1)

            def transposes(name, pieces):
                for j, piece in enumerate(pieces):
                    ins = nc.tensor.transpose(bank(name)[:, j * P:(j + 1) * P], piece, ident)
                ins.then_inc(psum_full, 1)

            def project(name):
                pe.wait_ge(chunk_in[name], 16)
                for t in range(TT):
                    free_bank(pe, f"{name}{t}")
                    for k in range(KC):
                        ins = mm(bank(f"{name}{t}"), uT[:, k, t * P:(t + 1) * P], chunk_ap(name)[:, k, :],
                                 start=(k == 0), stop=(k == KC - 1))
                    ins.then_inc(psum_full, 1)

            pe.wait_ge(const_in, 16)
            pe.wait_ge(xn_ready, TT)
            for g in range(4):
                transposes(f"uT{g}", [xn[:, t, k * P:(k + 1) * P] for k in (2 * g, 2 * g + 1) for t in range(TT)])
            pe.wait_ge(freed["act"], drained("uT2"))
            pe.wait_ge(freed["dve"], drained("uT3"))
            project("fq")

            pe.wait_ge(small_in, 16 * 5)
            for k in range(KC):
                ins = mm(bank("fz")[0:FOX_HEADS, 0:SEQ], w_z[:, k, :], uT[:, k, :], start=(k == 0), stop=(k == KC - 1))
            ins.then_inc(psum_full, 1)

            project("fk")
            pe.wait_ge(freed["act"], drained("fq1"))
            for t in range(TT):
                free_bank(pe, f"fqT{t}")
                transposes(f"fqT{t}", [fq[:, t, j * P:(j + 1) * P] for j in range(4)])
            project("rq")
            pe.wait_ge(freed["act"], drained("fk1"))
            for t in range(TT):
                free_bank(pe, f"fkT{t}")
                transposes(f"fkT{t}", [fk[:, t, j * P:(j + 1) * P] for j in range(4)])
            project("rk")

            pe.wait_ge(freed["dve"], drained("fqT1"))
            pe.wait_ge(freed["act"], drained("fkT1"))
            pe.wait_ge(fkz, 2)
            pe.wait_ge(aug_in, 32)
            for g, (t, h0, nh, keys) in enumerate(QK_GROUPS):
                free_bank(pe, f"qk{g}")
                tile = bank(f"qk{g}").rearrange("p (h s) -> p h s", h=nh)
                for j in range(nh):
                    h = h0 + j
                    kT = fkTo if h % 2 else fkTe
                    q = slice(t * P, (t + 1) * P)
                    mm(tile[:, j, :], fqT[:, h // 2, q], kT[:, h // 2, 0:keys], start=True, stop=False)
                    mm(tile[:, j, q], ident, causal, start=False, stop=False, skip_group_check=True)
                    ins = mm(tile[:, j, :], augq[0:2, h, q], augk[0:2, h, 0:keys], start=False, stop=True)
                ins.then_inc(psum_full, 1)

            project("fv")
            for name, src in (("rqT", rq), ("rkT", rk)):
                pe.wait_ge(dve_done, DVE_ROTATED)
                for t in range(TT):
                    free_bank(pe, f"{name}{t}")
                    transposes(f"{name}{t}", [src[:, t, h * P:(h + 1) * P] for h in range(RET_HEADS)])
            project("rv")
            pe.wait_ge(psum_full, full("fv1"))
            pe.sem_inc(w1_used, 2)
            for g, (t, s, h0) in enumerate(PT_GROUPS):
                pe.wait_ge(p_norm, 2 if t == 0 else 6)
                free_bank(pe, f"pT{g}")
                base, width = (0, P) if t == 0 else (TT * NW, SEQ)
                transposes(f"pT{g}", [p_w[:, base + h * width + s * P:base + h * width + s * P + P]
                                      for h in range(h0, h0 + 4)])

            pe.wait_ge(freed["dve"], drained("rqT1"))
            pe.wait_ge(freed["act"], drained("rkT1"))
            for h in range(RET_HEADS):
                free_bank(pe, f"rs{h}")
                mm(bank(f"rs{h}")[:, 0:SEQ], rkT[:, h, 0:P], rqT[:, h, :], start=True, stop=True)
                mm(bank(f"rs{h}")[:, SEQ:384], rkT[:, h, P:SEQ], rqT[:, h, P:SEQ], start=True, stop=True) \
                    .then_inc(psum_full, 1)
            pe.wait_ge(psum_full, full("rv1"))
            pe.sem_inc(w1_used, 2)
            project("rg")

            pe.wait_ge(freed["act"], drained("pT4"))
            pe.wait_ge(freed["dve"], drained("pT5"))
            for g in range(2):
                free_bank(pe, f"pv{g}")
                tile = bank(f"pv{g}").rearrange("p (j t) -> p j t", j=2)
                for jj in range(2):
                    for half in range(2):
                        h = 2 * (2 * g + jj) + half
                        rows = slice(half * FOX_D, (half + 1) * FOX_D)
                        v = slice(h * FOX_D, (h + 1) * FOX_D)
                        mm(tile[rows, jj, :], fv[:, 0, v], pT0[:, h, :], start=True, stop=True)
                        ins = mm(tile[rows, jj, P:SEQ], fv[:, 1, v], pT1[:, h, :], start=False, stop=True,
                                 skip_group_check=True)
                ins.then_inc(psum_full, 1)

            pe.wait_ge(psum_full, full("rg1"))
            pe.sem_inc(w1_used, 4)

            pe.wait_ge(freed["dve"], drained("rs3"))
            pe.wait_ge(freed["act"], drained("rv1"))
            for t in range(TT):
                free_bank(pe, f"ro{t}")
                for h in range(RET_HEADS):
                    d = slice(h * P, (h + 1) * P)
                    o = bank(f"ro{t}")[:, d]
                    if t == 0:
                        ins = mm(o, rsc[:, h, 0:P], rv[:, 0, d], start=True, stop=True)
                    else:
                        mm(o, rsc[:, h, P:SEQ], rv[:, 0, d], start=True, stop=False)
                        ins = mm(o, rsc[:, h, SEQ:384], rv[:, 1, d], start=False, stop=True)
                ins.then_inc(psum_full, 1)

            def out_chunk(j):
                for g in range(4):
                    t, n = g // 2, g % 2
                    ins = mm(bank(f"out{g}"), mixT[:, OUT_ORDER[j], t * P:(t + 1) * P],
                             w2[:, j, n * NW:(n + 1) * NW], start=(j == 0), stop=(j == KC - 1))
                    if j == KC - 1:
                        ins.then_inc(psum_full, 1)
                return ins

            for g in range(4):
                free_bank(pe, f"out{g}")
            pe.wait_ge(freed["act"], drained("pv1"))
            pe.wait_ge(wout_in[0], 16)
            for j in range(4):
                out_chunk(j).then_inc(w2_used, 1)
            for t in range(TT):
                pe.wait_ge(ron_ready, t + 1)
                free_bank(pe, f"rT{t}")
                transposes(f"rT{t}", [on[:, t, h * P:(h + 1) * P] for h in range(RET_HEADS)])
            pe.wait_ge(freed["act"], drained("rT1"))
            pe.wait_ge(wout_in[1], 16)
            for j in range(4, KC - 1):
                out_chunk(j).then_inc(w2_used, 1)
            out_chunk(KC - 1)

            pe.wait_ge(u_ready, TT)
            for g in range(4):
                free_bank(pe, f"vT{g}")
                transposes(f"vT{g}", [u[:, t, k * P:(k + 1) * P] for k in (2 * g, 2 * g + 1) for t in range(TT)])
            pe.wait_ge(freed["act"], drained("vT2"))
            pe.wait_ge(freed["dve"], drained("vT3"))
            free_bank(pe, "logits")
            for t in range(TT):
                for k in range(KC):
                    ins = mm(bank("logits")[:, t * EXPERTS:(t + 1) * EXPERTS], vT[:, k, t * P:(t + 1) * P],
                             w_rt[:, k, :], start=(k == 0), stop=(k == KC - 1))
            ins.then_inc(psum_full, 1)
            pe.wait_ge(picked_ready, 1)
            free_bank(pe, "pos")
            pos = bank("pos")
            mm(pos[:, 0:32], before, picked[:, 0, :], start=True, stop=True)
            mm(pos[:, 32:64], ones, picked[:, 0, :], start=True, stop=False)
            mm(pos[:, 32:64], before, picked[:, 1, :], start=False, stop=True)
            mm(pos[:, 64:96], ones, picked[:, 0, :], start=True, stop=False)
            mm(pos[:, 64:96], ones, picked[:, 1, :], start=False, stop=True).then_inc(psum_full, 1)
            pe.wait_ge(routed, 1)

            def gather():
                for k in range(KC):
                    n = 0
                    for s in range(3):
                        for t in range(TT):
                            ins = mm(psum[:, XT, k * SLOTS:(k + 1) * SLOTS], u_parts[:, s, t, k * P:(k + 1) * P],
                                     sel[:, t, :], start=(n == 0), stop=(n == 5))
                            n += 1
                ins.then_inc(gath_done, 1)

            def combine(t):
                for half in range(2):
                    ins = mm(psum[:, CB + half, :], cab[:, 2 * half + t, :], y, start=True, stop=True)
                ins.then_inc(comb_done, 1)

            def one_round(r):
                g0 = r * (EXPERTS + 1)
                pe.wait_ge(sel_ready, g0 + 1)
                gather()
                with pe.Fori(0, EXPERTS) as e:
                    i = r * EXPERTS + e
                    g = r * (EXPERTS + 1) + e
                    pe.wait_ge(xT_ready, g + 1)
                    pe.wait_ge(lc_ready, i + 1)
                    for k in range(KC):
                        pe.wait_ge(w1_in[k], 16 * i + 16)
                        for n in range(2):
                            for half in range(2):
                                cols = slice((2 * n + half) * NW, (2 * n + half + 1) * NW)
                                ins = mm(psum[half * 64:half * 64 + 64, H0 + n, :], xT[:, k, :], w1[:, k, cols],
                                         start=(k == 0), stop=False)
                        ins.then_inc(w1_used, 1)
                    pe.wait_ge(row_ready, i + 1)
                    for n in range(2):
                        for half in range(2):
                            cols = slice((2 * n + half) * NW, (2 * n + half + 1) * NW)
                            ins = mm(psum[half * 64:half * 64 + 64, H0 + n, :], sel_row[:, :],
                                     bias_rows[0:3 * EXPERTS, cols], start=False, stop=True)
                    ins.then_inc(h_ready, 1)

                    pe.wait_ge(y_ready, i + 1)
                    pe.wait_ge(cab_ready, i + r + 1)
                    pe.wait_ge(comb_added, 2 * g + 1)
                    combine(0)
                    pe.wait_ge(sel_ready, g + 2)
                    gather()
                    pe.wait_ge(gs_ready, i + 1)
                    for j in range(4):
                        ins = nc.tensor.transpose(psum[:, CT, j * P:(j + 1) * P],
                                                  gs[:, j % 2, (j // 2) * P:(j // 2 + 1) * P], ident)
                    ins.then_inc(cT_done, 1)
                    pe.wait_ge(a_ready, i + 1)
                    for j in range(4):
                        ins = nc.tensor.transpose(psum[:, AT, j * P:(j + 1) * P], act[:, j * P:(j + 1) * P], ident)
                    ins.then_inc(aT_done, 1)
                    pe.wait_ge(comb_added, 2 * g + 2)
                    combine(1)

                    for half in range(2):
                        ins = mm(psum[half * 64:half * 64 + 64, Y, :], sel_row[:, :],
                                 bias_rows[0:3 * EXPERTS, 2 * DM + half * NW:2 * DM + (half + 1) * NW],
                                 start=True, stop=False)
                    ins.then_inc(rows_used, 1)
                    pe.wait_ge(actT_ready, i + 1)
                    for k in range(KC):
                        pe.wait_ge(w2_in[k], 16 * i + 16)
                        for half in range(2):
                            lhs = actT[:, k % 4, (k // 4) * SLOTS:(k // 4 + 1) * SLOTS]
                            ins = mm(psum[half * 64:half * 64 + 64, Y, :], lhs, w2[:, k, half * NW:(half + 1) * NW],
                                     start=False, stop=(k == KC - 1))
                        if k < KC - 1:
                            ins.then_inc(w2_used, 1)
                    ins.then_inc(y_done, 1)
                pe.wait_ge(y_ready, (r + 1) * EXPERTS + 1)
                pe.wait_ge(cab_ready, (r + 1) * EXPERTS + r + 1)
                pe.wait_ge(comb_added, 2 * (g0 + EXPERTS) + 1)
                combine(0)
                pe.wait_ge(comb_added, 2 * (g0 + EXPERTS) + 2)
                combine(1)

            rounds(pe, one_round)

        @block.scalar
        def _(eng):
            eng.dma_start(const[:, :], table).then_inc(const_in, 16)
            eng.sem_inc(y_ready, 1)
            with nc.allow_non_contiguous_dma(reason="a gain per partition, 1024 words in all"):
                eng.dma_start(g_mix[:, :], norm_mix_g[0].rearrange("(k p) -> p k", p=P)).then_inc(small_in, 16)
            eng.dma_start(w_z[:, :, :], w_in_dram[:, :, FZ_COL:FZ_COL + FOX_HEADS]).then_inc(small_in, 16)
            eng.dma_start(b_fox[:, :], b_forget[0].rearrange("(p a) -> p a", a=1)).then_inc(small_in, 16)
            eng.dma_start(w_rt[:, :, :], w_router[0].rearrange("(k p) e -> p k e", p=P)).then_inc(small_in, 16)
            eng.dma_start(b_rt[:, :], b_router[0:1, :].to_broadcast([P, EXPERTS])).then_inc(small_in, 16)

            act_i = nc.scalar.activation

            def copy(o, i, scale=1.0):
                return act_i(o, i, ACT.Copy, scale=scale)

            eng.wait_ge(x_in, 16)
            for t in range(TT):
                act_i(xn[:, t, :], acc[:, t, :], ACT.Square, accum_out=ss[:, t:t + 1]).then_inc(sq_done, 1)

            def root_seeds(event):
                cols = ROOT_COLS[event]
                eng.wait_ge(root_ready, event + 1)
                act_i(root_log[:, cols], root_of[:, cols], ACT.Ln).then_inc(log_done, 1)
                eng.wait_ge(log_done, event + 1)
                act_i(inv_root[:, cols], root_log[:, cols], ACT.Exp, scale=-0.5).then_inc(seed_ready, 1)

            root_seeds(0)

            def scaled_uT(name, g):
                eng.wait_ge(psum_full, full(name))
                for j in range(2):
                    k = 2 * g + j
                    ins = copy(uT[:, k, :], bank(name)[:, j * SEQ:(j + 1) * SEQ], scale=g_mix[:, k:k + 1])
                ins.then_inc(freed["act"], 1)

            def read(name, o, i, scale=1.0):
                eng.wait_ge(psum_full, full(name))
                copy(o, i, scale).then_inc(freed["act"], 1)

            def four(name):
                return bank(name).rearrange("p (j t) -> p j t", j=4)

            eng.wait_ge(small_in, 16 * 5)
            scaled_uT("uT0", 0)
            scaled_uT("uT2", 2)
            for t in range(TT):
                read(f"fq{t}", fq[:, t, :], bank(f"fq{t}"), scale=FOX_D ** -0.5)
            z_neg, z_exp, z_log = zwork[0:FOX_HEADS, 1, :], zwork[0:FOX_HEADS, 2, :], zwork[0:FOX_HEADS, 3, :]
            eng.wait_ge(z_abs, 1)
            act_i(z_exp, z_neg, ACT.Exp).then_inc(act_done, 1)
            eng.wait_ge(act_done, 1)
            act_i(z_log, z_exp, ACT.Ln, bias=1.0).then_inc(z_ln, 1)
            for t in range(TT):
                read(f"fk{t}", fk[:, t, :], bank(f"fk{t}"))
            for t in range(TT):
                eng.wait_ge(psum_full, full(f"fkT{t}"))
                cols = slice(t * P, (t + 1) * P)
                copy(fkTe[0:FOX_D, :, cols], four(f"fkT{t}")[0:FOX_D, :, :])
                copy(fkTo[FOX_D:P, :, cols], four(f"fkT{t}")[FOX_D:P, :, :]).then_inc(freed["act"], 1)
            for g, (t, h0, nh, keys) in enumerate(QK_GROUPS):
                eng.wait_ge(max_ready, g + 1)
                base = 0 if t == 0 else TT * NW
                for j in range(nh):
                    h, col = h0 + j, t * FOX_HEADS + h0 + j
                    ins = act_i(p_w[:, base + h * keys:base + (h + 1) * keys], bank(f"qk{g}")[:, j * keys:(j + 1) * keys],
                                ACT.Exp, bias=negmax[:, col:col + 1], accum_out=psum_p[:, col:col + 1])
                ins.then_inc(freed["act"], 1)
            for t in range(TT):
                read(f"fv{t}", fv[:, t, :], bank(f"fv{t}"))
            for t in range(TT):
                read(f"rkT{t}", rkT[:, :, t * P:(t + 1) * P], four(f"rkT{t}"))
            for t in range(TT):
                read(f"rv{t}", rv[:, t, :], bank(f"rv{t}"))

            def read_pT(g):
                t, s, h0 = PT_GROUPS[g]
                dst = pT1[:, h0:h0 + 4, :] if s else pT0[:, h0:h0 + 4, t * P:(t + 1) * P]
                read(f"pT{g}", dst, four(f"pT{g}"))

            for g in (0, 2, 4):
                read_pT(g)
            for t in range(TT):
                eng.wait_ge(psum_full, full(f"rg{t}"))
                act_i(eg[:, t, :], bank(f"rg{t}"), ACT.Exp, scale=-1.0)
                copy(rg[:, t, :], bank(f"rg{t}")).then_inc(freed["act"], 1)
            for g in range(2):
                read(f"pv{g}", mixT[:, 4 + 2 * g:6 + 2 * g, :], bank(f"pv{g}").rearrange("p (j t) -> p j t", j=2))
            for t in range(TT):
                root_seeds(1 + t)
            for t in range(TT):
                read(f"rT{t}", mixT[:, 0:RET_HEADS, t * P:(t + 1) * P], four(f"rT{t}"))
            for t in range(TT):
                eng.wait_ge(h_done, t + 1)
                act_i(area("u")[:, t * DM:(t + 1) * DM], acc[:, t, :], ACT.Square,
                      accum_out=ss[:, TT + t:TT + t + 1]).then_inc(sq_done, 1)
                root_seeds(3 + t)
            eng.wait_ge(rows_ready, 2)
            for g in (0, 2):
                read(f"vT{g}", vT[:, 2 * g:2 * g + 2, :], bank(f"vT{g}").rearrange("p (k t) -> p k t", k=2))
            for t in range(TT):
                eng.wait_ge(topv_ready, t + 1)
                act_i(gate4[:, t, :], top_v[:, t, 0:TOP_K], ACT.Exp, bias=negtop[:, t:t + 1],
                      accum_out=gsum[:, t:t + 1]).then_inc(gexp_ready, 1)

            def read_xT():
                copy(xT[:, :, :], psum[:, XT, :].rearrange("p (k s) -> p k s", k=KC)).then_inc(xT_ready, 1)

            def one_round(r):
                g0 = r * (EXPERTS + 1)
                eng.wait_ge(gath_done, g0 + 1)
                read_xT()
                with eng.Fori(0, EXPERTS) as e:
                    i = r * EXPERTS + e
                    g = r * (EXPERTS + 1) + e
                    eng.wait_ge(gm_ready, i + 1)
                    act_i(sg, gm, ACT.Sigmoid, scale=ALPHA).then_inc(sg_ready, 1)
                    eng.wait_ge(gath_done, g + 2)
                    read_xT()
                    eng.wait_ge(aT_done, i + 1)
                    copy(actT[:, :, :], psum[:, AT, :].rearrange("p (j q) -> p j q", j=4)).then_inc(actT_ready, 1)
                    eng.wait_ge(cT_done, i + 2)
                    eng.wait_ge(comb_done, 2 * g + 2)
                    copy(cab[:, :, :], psum[:, CT, :].rearrange("p (j q) -> p j q", j=4)).then_inc(cab_ready, 1)
                    eng.wait_ge(y_done, i + 2)
                    copy(y, psum[:, Y, :]).then_inc(y_ready, 1)

            rounds(eng, one_round)
            for t in range(TT):
                eng.wait_ge(final_sq, t + 1)
                act_i(area("sq", TT, DM)[:, t, :], acc[:, t, :], ACT.Square, accum_out=ss[:, t:t + 1]).then_inc(sq_done, 1)
            root_seeds(5)

        @block.vector
        def _(dve):
            v = nc.vector
            steps = [0]
            for first in (lc_ready, comb_added):
                dve.sem_inc(first, 1)

            def then(ins):
                steps[0] += 1
                ins.then_inc(dve_done, 1)
                dve.wait_ge(dve_done, steps[0])

            def inverse_roots(event, square, scale, eps):
                cols = ROOT_COLS[event]
                w, r, t = root_of[:, cols], inv_root[:, cols], root_t[:, cols]
                dve.wait_ge(root_ready, event)
                v.tensor_scalar(w, square, scale, eps, ALU.mult, ALU.add).then_inc(root_ready, 1)
                dve.wait_ge(seed_ready, event + 1)
                then(v.tensor_tensor(t, r, r, ALU.mult))
                then(v.tensor_tensor(t, t, w, ALU.mult))
                then(v.tensor_scalar(t, t, -0.5, 1.5, ALU.mult, ALU.add))
                then(v.tensor_tensor(r, r, t, ALU.mult))

            v.memset(fkTe[FOX_D:P, :, :], 0.0).then_inc(fkz, 1)
            v.memset(fkTo[0:FOX_D, :, :], 0.0).then_inc(fkz, 1)
            v.memset(slot_of[:, :, :], -UNPICKED)
            v.memset(picked[:, :, :], 0.0)
            then(v.memset(gates[:, :, :], 0.0))
            dve.wait_ge(sq_done, TT)
            inverse_roots(0, ss[:, 0:TT], 1.0 / DM, RMS_EPS)
            for t in range(TT):
                v.tensor_scalar(xn[:, t, :], acc[:, t, :], inv_root[:, t:t + 1], None, ALU.mult).then_inc(xn_ready, 1)

            dve.wait_ge(small_in, 16 * 5)
            for name, g in (("uT1", 1), ("uT3", 3)):
                dve.wait_ge(psum_full, full(name))
                for j in range(2):
                    k = 2 * g + j
                    ins = v.tensor_scalar(uT[:, k, :], bank(name)[:, j * SEQ:(j + 1) * SEQ], g_mix[:, k:k + 1],
                                          None, ALU.mult)
                ins.then_inc(freed["dve"], 1)

            zb, zneg, zlog, zls, zf, znf = (zwork[0:FOX_HEADS, j, :] for j in (0, 1, 3, 4, 5, 6))
            dve.wait_ge(psum_full, full("fz"))
            v.tensor_scalar(zb, bank("fz")[0:FOX_HEADS, 0:SEQ], b_fox[:, 0:1], None, ALU.add).then_inc(freed["dve"], 1)
            dve.wait_ge(freed["dve"], drained("fz"))
            v.scalar_tensor_tensor(out=zneg, in0=zb, scalar=-1.0, in1=zb, op0=ALU.mult, op1=ALU.min).then_inc(z_abs, 1)
            dve.wait_ge(z_ln, 1)
            then(v.scalar_tensor_tensor(out=zls, in0=zb, scalar=0.0, in1=zlog, op0=ALU.min, op1=ALU.subtract))
            dve.wait_ge(const_in, 16)
            v.tensor_tensor_scan(zf, const[0:FOX_HEADS, CONST_AT["ones"][0]:CONST_AT["ones"][0] + 1].to_broadcast([FOX_HEADS, SEQ]),
                                 zls, 0.0, ALU.mult, ALU.add).then_inc(gate_f, 1)
            dve.wait_ge(gate_f, 1)
            v.tensor_scalar(znf, zf, -1.0, None, ALU.mult).then_inc(neg_f, 1)

            def four(name):
                return bank(name).rearrange("p (j t) -> p j t", j=4)

            def read(name, o, i):
                dve.wait_ge(psum_full, full(name))
                v.tensor_copy(o, i).then_inc(freed["dve"], 1)

            for t in range(TT):
                read(f"fqT{t}", fqT[:, :, t * P:(t + 1) * P], four(f"fqT{t}"))

            def rotate(name, dst, t):
                dve.wait_ge(psum_full, full(name))
                src = bank(name).rearrange("p (h a j) -> p h a j", h=RET_HEADS, a=2)
                part = rot[:, 0, :].rearrange("p (h a j) -> p h a j", h=RET_HEADS, a=2)
                turn = rot[:, 1, :].rearrange("p (h a j) -> p h a j", h=RET_HEADS, a=2)
                shape = [P, RET_HEADS, 64]
                for a in range(2):
                    v.tensor_tensor(part[:, :, a, :], src[:, :, a, :], cos[:, t:t + 1, :].to_broadcast(shape), ALU.mult)
                v.tensor_tensor(turn[:, :, 0, :], src[:, :, 1, :], negsin[:, t:t + 1, :].to_broadcast(shape), ALU.mult)
                v.tensor_tensor(turn[:, :, 1, :], src[:, :, 0, :], sin[:, t:t + 1, :].to_broadcast(shape), ALU.mult) \
                    .then_inc(freed["dve"], 1)
                dve.wait_ge(freed["dve"], drained(name))
                then(v.tensor_tensor(dst[:, t, :], rot[:, 0, :], rot[:, 1, :], ALU.add))

            for name, dst in (("rq", rq), ("rk", rk)):
                for t in range(TT):
                    rotate(f"{name}{t}", dst, t)
            assert steps[0] == DVE_ROTATED

            for g, (t, h0, nh, keys) in enumerate(QK_GROUPS):
                dve.wait_ge(psum_full, full(f"qk{g}"))
                col = t * FOX_HEADS + h0
                v.tensor_reduce(negmax[:, col:col + nh], bank(f"qk{g}").rearrange("p (h s) -> p h s", h=nh),
                                AX.X, ALU.max, negate=True).then_inc(max_ready, 1)
            for g, (t, h0, nh, keys) in enumerate(QK_GROUPS):
                dve.wait_ge(freed["act"], drained(f"qk{g}"))
                col = t * FOX_HEADS + h0
                base = (0 if t == 0 else TT * NW) + h0 * keys
                tile = p_w[:, base:base + nh * keys].rearrange("p (h s) -> p h s", h=nh)
                then(v.reciprocal(rsum_p[:, col:col + nh], psum_p[:, col:col + nh]))
                scale = rsum_p[:, col:col + nh].rearrange("p (h a) -> p h a", a=1).to_broadcast([P, nh, keys])
                v.tensor_tensor(tile, tile, scale, ALU.mult).then_inc(p_norm, 1)
            for t in range(TT):
                read(f"rqT{t}", rqT[:, :, t * P:(t + 1) * P], four(f"rqT{t}"))
            for g in (1, 3, 5):
                t, s, h0 = PT_GROUPS[g]
                dst = pT1[:, h0:h0 + 4, :] if s else pT0[:, h0:h0 + 4, t * P:(t + 1) * P]
                read(f"pT{g}", dst, four(f"pT{g}"))
            for h in range(RET_HEADS):
                dve.wait_ge(psum_full, full(f"rs{h}"))
                v.tensor_tensor(rsc[:, h, :], bank(f"rs{h}")[:, 0:384], decay[:, h, :], ALU.mult) \
                    .then_inc(freed["dve"], 1)
            dve.wait_ge(freed["act"], drained("rg1"))
            then(v.tensor_scalar(area("eg"), area("eg"), 1.0, None, ALU.add))
            then(v.reciprocal(area("eg"), area("eg")))
            then(v.tensor_tensor(area("rg"), area("rg"), area("eg"), ALU.mult))
            for t in range(TT):
                dve.wait_ge(psum_full, full(f"ro{t}"))
                tile = bank(f"ro{t}").rearrange("p (h d) -> p h d", h=RET_HEADS)
                for h in range(RET_HEADS):
                    ins = v.bn_stats(stats[:, h, :], tile[:, h, :])
                then(ins)
                for h in range(RET_HEADS):
                    ins = v.bn_aggr(mv[:, h, :], stats[:, h, :])
                then(ins)
                inverse_roots(1 + t, mv[:, :, 1], 1.0, GN_EPS)
                for h in range(RET_HEADS):
                    ins = v.tensor_scalar(on[:, t, h * P:(h + 1) * P], tile[:, h, :], mv[:, h, 0:1],
                                          inv_root[:, ROOT_COLS[1 + t].start + h:ROOT_COLS[1 + t].start + h + 1], ALU.subtract, ALU.mult)
                ins.then_inc(freed["dve"], 1)
                dve.wait_ge(freed["dve"], drained(f"ro{t}"))
                v.tensor_tensor(on[:, t, :], on[:, t, :], rg[:, t, :], ALU.mult).then_inc(ron_ready, 1)
            for g in range(4):
                t, n = g // 2, g % 2
                dve.wait_ge(psum_full, full(f"out{g}"))
                cols = slice(n * NW, (n + 1) * NW)
                v.tensor_tensor(acc[:, t, cols], acc[:, t, cols], bank(f"out{g}"), ALU.add).then_inc(freed["dve"], 1)
                if n == 1:
                    dve.wait_ge(freed["dve"], drained(f"out{g}"))
                    dve.sem_inc(h_done, 1)
            dve.wait_ge(gains_in, 32)
            for t in range(TT):
                dve.wait_ge(sq_done, TT + t + 1)
                inverse_roots(3 + t, ss[:, TT + t:TT + t + 1], 1.0 / DM, RMS_EPS)
                v.scalar_tensor_tensor(out=u[:, t, :], in0=acc[:, t, :], scalar=inv_root[:, ROOT_COLS[3 + t]],
                                       in1=area("g_ffn"), op0=ALU.mult, op1=ALU.mult).then_inc(u_ready, 1)
            dve.wait_ge(rows_ready, 2)
            for g in (1, 3):
                read(f"vT{g}", vT[:, 2 * g:2 * g + 2, :], bank(f"vT{g}").rearrange("p (k t) -> p k t", k=2))
            uf, rest = area("u"), area("u_rest")
            parts = [u_parts[:, s, :, :].rearrange("p t d -> p (t d)") for s in range(3)]
            then(v.tensor_copy(parts[0], uf))
            then(v.tensor_tensor(rest, uf, parts[0], ALU.subtract))
            then(v.tensor_copy(parts[1], rest))
            then(v.tensor_tensor(parts[2], rest, parts[1], ALU.subtract))

            dve.wait_ge(psum_full, full("logits"))
            for t in range(TT):
                ins = v.tensor_tensor(logits[:, t, :], bank("logits")[:, t * EXPERTS:(t + 1) * EXPERTS], b_rt[:, :], ALU.add)
            ins.then_inc(freed["dve"], 1)
            dve.wait_ge(freed["dve"], drained("logits"))
            for t in range(TT):
                then(v.max(top_v[:, t, :], logits[:, t, :]))
                v.max_index(top_i[:, t, :], top_v[:, t, :], logits[:, t, :])
                v.tensor_scalar(negtop[:, t:t + 1], top_v[:, t, 0:1], -1.0, None, ALU.mult).then_inc(topv_ready, 1)
            dve.wait_ge(topv_ready, TT)
            then(v.tensor_copy(top_f[:, :, :], top_i[:, :, 0:TOP_K]))
            for t in range(TT):
                dve.wait_ge(gexp_ready, t + 1)
                then(v.reciprocal(gsum[:, t:t + 1], gsum[:, t:t + 1]))
                then(v.tensor_scalar(gate4[:, t, :], gate4[:, t, :], gsum[:, t:t + 1], None, ALU.mult))
                for j in range(TOP_K):
                    then(v.tensor_scalar(onehot[:, :], expert_ids, top_f[:, t, j:j + 1], None, ALU.is_equal))
                    v.tensor_tensor(picked[:, t, :], picked[:, t, :], onehot[:, :], ALU.add)
                    then(v.scalar_tensor_tensor(out=gates[:, t, :], in0=onehot[:, :], scalar=gate4[:, t, j:j + 1],
                                                in1=gates[:, t, :], op0=ALU.mult, op1=ALU.add))
            dve.sem_inc(picked_ready, 1)
            dve.wait_ge(psum_full, full("pos"))
            pos = bank("pos")
            for t in range(TT):
                then(v.scalar_tensor_tensor(out=slot_of[:, t, 0:EXPERTS], in0=pos[:, t * EXPERTS:(t + 1) * EXPERTS],
                                            scalar=UNPICKED, in1=picked[:, t, :], op0=ALU.add, op1=ALU.mult))
            then(v.tensor_scalar(slot_of[:, :, 0:EXPERTS], slot_of[:, :, 0:EXPERTS], UNPICKED, None, ALU.subtract))
            then(v.memset(cab[:, :, :], 0.0))
            then(v.memset(y, 0.0))
            dve.sem_inc(cab_ready, 1)
            v.tensor_reduce(most[0:1, 0:1], pos[0:1, 64:96], AX.X, ALU.max).then_inc(routed, 1)
            def select(e):
                for t in range(TT):
                    ins = v.tensor_scalar(sel[:, t, :], slot_ids[:, 0:SLOTS], slot_of[:, t, bass.ds(e, 1)], None, ALU.is_equal)
                ins.then_inc(sel_ready, 1)

            def add_combined(t):
                v.tensor_tensor(acc[:, t, :], acc[:, t, :], psum[:, CB:CB + 2, :].rearrange("p b n -> p (b n)"),
                                ALU.add).then_inc(comb_added, 1)

            def one_round(r):
                g0 = r * (EXPERTS + 1)
                dve.wait_ge(cab_ready, g0 + 1)
                select(0)
                with dve.Fori(0, EXPERTS) as e:
                    i = r * EXPERTS + e
                    g = r * (EXPERTS + 1) + e
                    dve.wait_ge(gath_done, g + 1)
                    select(e + 1)
                    dve.wait_ge(cT_done, i + 1)
                    for t in range(TT):
                        ins = v.tensor_scalar(gs[:, t, :], slot_ids, slot_of[:, t, bass.ds(e, 1)],
                                              gates[:, t, bass.ds(e, 1)], ALU.is_equal, ALU.mult)
                    ins.then_inc(gs_ready, 1)
                    dve.wait_ge(rows_used, i + 1)
                    v.tensor_scalar(sel_row[:, :], ones[0:3 * EXPERTS, 0:SLOTS], piece_row[0:3 * EXPERTS, bass.ds(e, 1)],
                                    None, ALU.mult).then_inc(row_ready, 1)
                    dve.wait_ge(h_ready, i + 1)
                    v.tensor_scalar(gm, psum[:, H0, :], LIMIT, None, ALU.min).then_inc(gm_ready, 1)
                    v.tensor_scalar(lc, psum[:, H1, :], LIMIT, -LIMIT, ALU.min, ALU.max).then_inc(lc_ready, 1)
                    dve.wait_ge(lc_ready, i + 2)
                    v.scalar_tensor_tensor(out=lg, in0=lc, scalar=1.0, in1=gm, op0=ALU.add, op1=ALU.mult) \
                        .then_inc(lg_ready, 1)
                    dve.wait_ge(lg_ready, i + 1)
                    dve.wait_ge(sg_ready, i + 1)
                    v.tensor_tensor(act, lg, sg, ALU.mult).then_inc(a_ready, 1)
                    for t in range(TT):
                        dve.wait_ge(comb_done, 2 * g + t + 1)
                        add_combined(t)
                for t in range(TT):
                    dve.wait_ge(comb_done, 2 * (g0 + EXPERTS) + t + 1)
                    add_combined(t)
                dve.wait_ge(comb_added, 2 * (g0 + EXPERTS + 1) + 1)
                v.memset(cab[:, :, :], 0.0)
                v.tensor_scalar(slot_of[:, :, :], slot_of[:, :, :], float(SLOTS), None, ALU.subtract).then_inc(cab_ready, 1)

            rounds(dve, one_round)

            for t in range(TT):
                dve.sem_inc(final_sq, 1)
            dve.wait_ge(sq_done, 3 * TT)
            inverse_roots(5, ss[:, 0:TT], 1.0 / DM, RMS_EPS)
            for t in range(TT):
                ins = v.scalar_tensor_tensor(out=acc[:, t, :], in0=acc[:, t, :],
                                             scalar=inv_root[:, ROOT_COLS[5].start + t:ROOT_COLS[5].start + t + 1],
                                             in1=area("g_final"), op0=ALU.mult, op1=ALU.mult)
            ins.then_inc(final_ready, 1)


DVE_ROTATED = 10

_INS = ["x", "norm_mix_g", "w_in", "b_forget", "w_out", "norm_ffn_g", "w_router", "b_router",
        "w_exp_in", "b_exp_in", "w_exp_out", "b_exp_out", "norm_final_g"]


def kernel(**inputs):
    import numpy as _np
    import concourse.bacc as _bacc
    from concourse import mybir as _mybir
    from concourse.bass_utils import run_bass_kernel_spmd as _run

    nc = _bacc.Bacc("TRN2", target_bir_lowering=False, num_devices=1)
    arrays, args = {}, []
    given = [(name, _np.ascontiguousarray(inputs[name])) for name in _INS] + [("table", constant_table())]
    for name, a in given:
        arrays[f"in_{name}"] = a
        args.append(nc.dram_tensor(f"in_{name}", a.shape, _mybir.dt.from_np(a.dtype), kind="ExternalInput").ap())
    o = nc.dram_tensor("out_0", (1, SEQ, DM), _mybir.dt.float32, kind="ExternalOutput").ap()
    build(nc, *args, o)
    r = _run(nc, [arrays], core_ids=[0])
    return r.results[0]["out_0"]
```

```python
from contextlib import ExitStack

import numpy as np

import concourse.bass as bass
from concourse import mybir

F32 = mybir.dt.float32
BF16 = mybir.dt.bfloat16
I32 = mybir.dt.int32
U32 = mybir.dt.uint32
ALU = mybir.AluOpType
ACT = mybir.ActivationFunctionType
AX = mybir.AxisListType

P = 128
SEQ, DM = 256, 1024
TT = SEQ // P
KC = DM // P
NW = 512
RET_HEADS, RET_D = 4, 128
FOX_HEADS, FOX_D = 8, 64
CHUNK = 64
EXPERTS, TOP_K = 32, 4
SLOTS = 64
ROUNDS = SEQ // SLOTS
UNPICKED = 1024.0
RMS_EPS = GN_EPS = 1e-5
LIMIT, ALPHA = 7.0, 1.702
MASKED = -1e30

CONST_COLS = [("ident", P), ("before", P), ("ones", P), ("causal", P), ("cos", TT * 64),
              ("sin", TT * 64), ("negsin", TT * 64), ("decay", RET_HEADS * 384),
              ("slot_ids", 4 * SLOTS), ("expert_ids", EXPERTS), ("piece_row", EXPERTS + 2)]
CONST_AT = {}
_n = 0
for _name, _w in CONST_COLS:
    CONST_AT[_name] = (_n, _w)
    _n += _w
CONST_W = _n


def constant_table():
    t = np.zeros((P, CONST_W), np.float32)

    def put(name, a):
        at, w = CONST_AT[name]
        t[:a.shape[0], at:at + w] = a.reshape(a.shape[0], w)

    i = np.arange(P)
    put("ident", np.eye(P, dtype=np.float32))
    put("before", (i[:, None] < i[None, :]).astype(np.float32))
    put("ones", np.ones((P, P), np.float32))
    put("causal", np.where(i[None, :] <= i[:, None], 0.0, MASKED).astype(np.float32))
    half = RET_D // 2
    freq = np.float32(10000.0) ** (-np.arange(half, dtype=np.float32) / np.float32(half))
    angle = (np.arange(SEQ, dtype=np.float32)[:, None] * freq[None, :]).reshape(TT, P, half)
    angle = angle.transpose(1, 0, 2).astype(np.float64)
    put("cos", np.cos(angle).astype(np.float32))
    put("sin", np.sin(angle).astype(np.float32))
    put("negsin", -np.sin(angle).astype(np.float32))
    log_gamma = np.log1p(-np.exp2(-5.0 - np.arange(RET_HEADS)))
    dec = np.zeros((P, RET_HEADS, 384))
    for key0, query0, at, n in ((0, 0, 0, SEQ), (P, P, SEQ, P)):
        s = key0 + i[:, None]
        q = query0 + np.arange(n)[None, :]
        seen = s // CHUNK <= q // CHUNK
        for h in range(RET_HEADS):
            dec[:, h, at:at + n] = np.where(seen, np.exp(log_gamma[h] * np.abs(q - s)), 0.0)
    put("decay", (dec * RET_D ** -0.5).astype(np.float32))
    ids = np.arange(SLOTS)
    none = np.full(SLOTS, 0.5)
    put("slot_ids", np.broadcast_to(np.concatenate([ids, none, none, ids]), (P, 4 * SLOTS)).astype(np.float32))
    put("expert_ids", np.broadcast_to(np.arange(EXPERTS), (P, EXPERTS)).astype(np.float32))
    rows = np.zeros((P, EXPERTS + 2), np.float32)
    rows[:3 * EXPERTS, :EXPERTS] = np.tile(np.eye(EXPERTS), (3, 1))
    put("piece_row", rows)
    return t


GROUPS = (
    [("gT", "act"), ("uT0", "act"), ("uT1", "dve"), ("uT2", "act"), ("uT3", "dve")]
    + [("fq0", "act"), ("fq1", "act"), ("fz", "dve"), ("fk0", "act"), ("fk1", "act")]
    + [("fqT0", "dve"), ("fqT1", "dve")]
    + [("rq0", "dve"), ("rq1", "dve"), ("fkT0", "act"), ("fkT1", "act")]
    + [("rk0", "dve"), ("rk1", "dve")]
    + [(f"qk{g}", "act") for g in range(6)]
    + [("fv0", "act"), ("fv1", "act")]
    + [("rqT0", "dve"), ("rqT1", "dve"), ("rkT0", "act"), ("rkT1", "act")]
    + [("rv0", "act"), ("rv1", "act")]
    + [(f"pT{g}", "dve" if g % 2 else "act") for g in range(6)]
    + [(f"rs{h}", "dve") for h in range(RET_HEADS)]
    + [("rg0", "act"), ("rg1", "act"), ("pv0", "act"), ("pv1", "act")]
    + [("ro0", "dve"), ("ro1", "dve"), ("rT0", "act"), ("rT1", "act")]
    + [(f"out{g}", "dve") for g in range(4)]
    + [("vT00", "act"), ("vT01", "act"), ("logits0", "dve")]
    + [("vT10", "act"), ("vT11", "dve"), ("logits1", "dve"), ("pos", "dve")]
)
GROUP_AT = {name: n for n, (name, _) in enumerate(GROUPS)}
BANKS = 8

QK_GROUPS = [(0, 0, 4, P), (0, 4, 4, P)] + [(1, 2 * j, 2, SEQ) for j in range(4)]
PT_GROUPS = [(0, 0, 0), (0, 0, 4), (1, 0, 0), (1, 0, 4), (1, 1, 0), (1, 1, 4)]

CHUNKS = [("fq", 2048, 0), ("fk", 2560, 1), ("rq", 0, 2), ("rk", 512, 3),
          ("fv", 3072, 0), ("rv", 1024, 1), ("rg", 1536, 2)]
FZ_COL = 3584
SLOT_OF = {name: s for name, _, s in CHUNKS}
OUT_ORDER = [4, 5, 6, 7, 0, 1, 2, 3]

ARENA = {
    "uT": (0, 2048), "xn": (2048, 2048), "fq": (4096, 1024), "p": (2048, 3072),
    "fk": (5120, 1024), "rq": (6144, 1024), "rk": (7168, 1024), "pT": (5120, 3072),
    "fqT": (8192, 1024), "fkTe": (9216, 1024), "fkTo": (10240, 1024),
    "fv": (11264, 1024), "zwork": (11264, 1792), "z_parts": (13056, 768),
    "rqT": (12288, 1024), "rkT": (13312, 1024),
    "rv": (14336, 1024), "rg": (15360, 1024), "augq": (14336, 1024), "augk": (15360, 1024),
    "eg": (16384, 1024), "on": (17408, 1024),
    "rot": (18432, 1024), "rsc": (18432, 1536),
    "g_ffn": (0, 1024), "g_final": (1024, 1024),
    "bias": (8192, 3072), "bias_rest": (2048, 3072), "bias_rows": (11264, 1536), "bias_part": (12800, 1536),
    "u": (5120, 2048), "u_rest": (2048, 2048), "u_parts": (16384, 3072), "vT": (14336, 2048),
    "xT": (8192, 512), "gm": (8704, 512), "lc": (9216, 512), "lg": (9728, 512), "sg": (10240, 512),
    "act": (10752, 512), "actT": (4096, 512), "cab": (4608, 512), "gs": (7168, 512), "y": (7680, 512),
    "onehot": (12800, 256), "gated": (13056, 256), "result": (5120, 2048),
}
ARENA_W = 19968
ROOT_COLS = [slice(0, 2), slice(2, 6), slice(6, 10), slice(10, 11), slice(11, 12), slice(12, 14)]
RING_W2 = KC * 2 * DM
RING_W = RING_W2 + KC * DM


def build(nc, x, norm_mix_g, w_in, b_forget, w_out, norm_ffn_g, w_router, b_router,
          w_exp_in, b_exp_in, w_exp_out, b_exp_out, norm_final_g, table, out):
    with ExitStack() as ctx:
        def sb(name, shape, dt=F32):
            return ctx.enter_context(nc.sbuf_tensor(name, shape, dt))

        def sem(name):
            return ctx.enter_context(nc.semaphore(name))

        ring = sb("ring", [P, RING_W])
        arena = sb("arena", [P, ARENA_W])
        const = sb("const", [P, CONST_W])
        acc = sb("acc", [P, TT, DM])
        mixT = sb("mixT", [P, KC, SEQ])
        w_z = sb("w_z", [P, KC, FOX_HEADS])
        g_rows = sb("g_rows", [KC, P])
        g_mix = sb("g_mix", [P, KC])
        ident_h = sb("ident_h", [P, P], BF16)
        before_h = sb("before_h", [P, P], BF16)
        ones_h = sb("ones_h", [P, P], BF16)
        causal_h = sb("causal_h", [P, P], BF16)
        b_fox = sb("b_fox", [FOX_HEADS, 1])
        w_rt = sb("w_rt", [P, KC, EXPERTS])
        b_rt = sb("b_rt", [P, EXPERTS])
        ss = sb("ss", [P, 2 * TT])
        negmax = sb("negmax", [P, TT * FOX_HEADS])
        psum_p = sb("psum_p", [P, TT * FOX_HEADS])
        rsum_p = sb("rsum_p", [P, TT * FOX_HEADS])
        stats = sb("stats", [P, RET_HEADS, 6])
        mv = sb("mv", [P, RET_HEADS, 2])
        root_of = sb("root_of", [P, 14])
        inv_root = sb("inv_root", [P, 14])
        root_t = sb("root_t", [P, 14])
        root_sqrt = sb("root_sqrt", [P, 14])
        logits = sb("logits", [P, TT, EXPERTS])
        top_v = sb("top_v", [P, TT, 8])
        top_i = sb("top_i", [P, TT, 8], U32)
        gate4 = sb("gate4", [P, TT, TOP_K])
        gsum = sb("gsum", [P, TT])
        negtop = sb("negtop", [P, TT])
        picked = sb("picked", [P, TT, EXPERTS], BF16)
        unpicked = sb("unpicked", [P, TT, EXPERTS])
        gates = sb("gates", [P, TT, EXPERTS])
        slot_of = sb("slot_of", [P, TT, EXPERTS + 2])
        most = sb("most", [1, 1], I32)
        sel = sb("sel", [P, TT, SLOTS], BF16)
        sel_row = sb("sel_row", [3 * EXPERTS, SLOTS], BF16)
        psum = ctx.enter_context(nc.psum_tensor("psum", [P, BANKS, NW], F32))

        def area(name, *shape):
            at, w = ARENA[name]
            v = arena[:, at:at + w]
            if len(shape) == 2:
                v = v.rearrange("p (a b) -> p a b", a=shape[0])
            if len(shape) == 3:
                v = v.rearrange("p (a b c) -> p a b c", a=shape[0], b=shape[1])
            return v

        def c(name):
            at, w = CONST_AT[name]
            return const[:, at:at + w]

        ident, before, ones, causal = c("ident"), c("before"), c("ones"), c("causal")
        cos, sin, negsin = (c(n).rearrange("p (t j) -> p t j", t=TT) for n in ("cos", "sin", "negsin"))
        decay = c("decay").rearrange("p (h j) -> p h j", h=RET_HEADS)
        slot_ids, expert_ids, piece_row = c("slot_ids"), c("expert_ids"), c("piece_row")

        uT = area("uT", KC, SEQ)
        xn = area("xn", TT, DM)
        fq, fk, fv = (area(n, TT, NW) for n in ("fq", "fk", "fv"))
        rq, rk, rv, rg, eg, on = (area(n, TT, NW) for n in ("rq", "rk", "rv", "rg", "eg", "on"))
        fqT, fkTe, fkTo = (area(n, 4, SEQ) for n in ("fqT", "fkTe", "fkTo"))
        rqT, rkT = (area(n, RET_HEADS, SEQ) for n in ("rqT", "rkT"))
        rot = area("rot", 2, NW)
        rsc = area("rsc", RET_HEADS, 384)
        augq, augk = (area(n).bitcast(BF16).rearrange("p (h t) -> p h t", h=FOX_HEADS) for n in ("augq", "augk"))
        zwork = area("zwork", 7, SEQ)
        z_parts = area("z_parts").bitcast(BF16)[0:FOX_HEADS, :].rearrange("p (s t) -> p s t", s=6)
        onehot, gated = (area(n).rearrange("p (t j e) -> p t j e", t=TT, j=TOP_K) for n in ("onehot", "gated"))
        p_w, pT_w = area("p"), area("pT")
        pT0 = pT_w[:, 0:2048].rearrange("p (h t) -> p h t", h=FOX_HEADS)
        pT1 = pT_w[:, 2048:3072].rearrange("p (h t) -> p h t", h=FOX_HEADS)
        vT = area("vT", KC, SEQ)
        u = area("u", TT, DM)
        u_rest = area("u_rest", TT, DM)
        u_parts = area("u_parts").bitcast(BF16).rearrange("p (s t d) -> p s t d", s=3, t=TT)
        bias, bias_rest = area("bias"), area("bias_rest")
        bias_rows, bias_part = area("bias_rows").bitcast(BF16), area("bias_part").bitcast(BF16)
        xT = area("xT", KC, SLOTS)
        gm, lc, lg, sg, act, y = (area(n) for n in ("gm", "lc", "lg", "sg", "act", "y"))
        actT, cab = area("actT", 4, P), area("cab", 4, P)
        gs = area("gs", TT, 4 * SLOTS)
        result = area("result", TT, DM)
        w1 = ring[:, 0:RING_W2].rearrange("p (k n) -> p k n", k=KC)
        w2 = ring[:, RING_W2:].rearrange("p (k n) -> p k n", k=KC)

        def chunk_ap(name):
            s = SLOT_OF[name]
            return ring[:, s * KC * NW:(s + 1) * KC * NW].rearrange("p (k n) -> p k n", k=KC)

        x_in, const_in, tables_in, gain_in, small_in = ([sem(f"x_in{t}") for t in range(TT)], sem("const_in"),
                                                        sem("tables_in"), sem("gain_in"), sem("small_in"))
        halves_ready = sem("halves_ready")
        chunk_in = {name: sem(f"{name}_in") for name, _, _ in CHUNKS}
        wout_in = [sem(f"wout_in{j}") for j in range(2)]
        bias_in, gains_in, aug_in = sem("bias_in"), sem("gains_in"), sem("aug_in")
        psum_full = sem("psum_full")
        freed = {"act": sem("freed_by_act"), "dve": sem("freed_by_dve")}
        dve_done, act_done = sem("dve_done"), sem("act_done")
        xn_ready, aug_zero, gate_f, neg_f = sem("xn_ready"), sem("aug_zero"), sem("gate_f"), sem("neg_f")
        z_abs, z_ln = sem("z_abs"), sem("z_ln")
        max_ready, p_ready, p_norm = sem("max_ready"), sem("p_ready"), sem("p_norm")
        fkz = sem("fkz")
        ron_ready, h_done, sq_done = sem("ron_ready"), sem("h_done"), sem("sq_done")
        u_ready, rows_ready, pool_done = sem("u_ready"), sem("rows_ready"), sem("pool_done")
        topv_ready, gexp_ready, picked_ready, routed = (
            sem("topv_ready"), sem("gexp_ready"), sem("picked_ready"), sem("routed"))
        w1_in = [sem(f"w1_in{k}") for k in range(KC)]
        w2_in = [sem(f"w2_in{k}") for k in range(KC)]
        w1_used, w2_used = sem("w1_used"), sem("w2_used")
        sel_ready, gath_done, xT_ready = sem("sel_ready"), sem("gath_done"), sem("xT_ready")
        row_ready, rows_used = sem("row_ready"), sem("rows_used")
        h_ready, gm_ready, lc_ready, lg_ready, sg_ready, a_ready = (
            sem("h_ready"), sem("gm_ready"), sem("lc_ready"), sem("lg_ready"), sem("sg_ready"), sem("a_ready"))
        aT_done, actT_ready, gs_ready, cT_done, cab_ready = (
            sem("aT_done"), sem("actT_ready"), sem("gs_ready"), sem("cT_done"), sem("cab_ready"))
        y_done, y_ready, comb_done, comb_added = sem("y_done"), sem("y_ready"), sem("comb_done"), sem("comb_added")
        root_ready, seed_ready = sem("root_ready"), sem("seed_ready")
        moved, stored, round_stored = sem("moved"), sem("stored"), sem("round_stored")
        final_sq, final_w, final_seed, final_step, final_ready = (
            sem("final_sq"), sem("final_w"), sem("final_seed"), sem("final_step"), sem("final_ready"))

        x_dram = x[0].rearrange("(t p) d -> p t d", p=P)
        out_dram = out[0].rearrange("(t p) d -> p t d", p=P)
        w_in_dram = w_in[0].rearrange("(k p) n -> p k n", p=P)
        w_out_dram = w_out[0].rearrange("(k p) n -> p k n", p=P)

        def bank(name):
            return psum[:, GROUP_AT[name] % BANKS, :]

        def drained(name):
            n = GROUP_AT[name]
            return sum(1 for _, e in GROUPS[:n + 1] if e == GROUPS[n][1])

        def full(name):
            return GROUP_AT[name] + 1

        def free_bank(eng, name):
            n = GROUP_AT[name] - BANKS
            if n >= 0:
                before_name, reader = GROUPS[n]
                eng.wait_ge(freed[reader], drained(before_name))

        Y = GROUP_AT["pos"] % BANKS
        H0, CB = [b for b in range(0, BANKS, 2) if Y not in (b, b + 1)][:2]
        H1 = H0 + 1
        XT, CT, AT = [b for b in range(BANKS) if b not in (Y, H0, H1, CB, CB + 1)]

        block = ctx.enter_context(nc.Block())

        def rounds(eng, body):
            need = eng.alloc_register(f"need_{eng.engine.name}")
            eng.reg_mov(need, SLOTS)
            with eng.Fori(0, ROUNDS) as r:
                with eng.If(eng.snap(need) > r * SLOTS):
                    body(r)
                    eng.wait_ge(routed, 1)
                    eng.reg_load(need, most[0:1, 0:1])

        @block.sync
        def _(sp):
            def load_chunk(name):
                col = {n: cc for n, cc, _ in CHUNKS}[name]
                sp.dma_start(chunk_ap(name), w_in_dram[:, :, col:col + NW]).then_inc(chunk_in[name], 16)

            for t in range(TT):
                sp.dma_start(acc[:, t, :], x_dram[:, t, :]).then_inc(x_in[t], 16)
            for name in ("fq", "fk", "rq", "rk"):
                load_chunk(name)
            for j in range(2):
                k0 = OUT_ORDER[4 * j]
                sp.dma_start(w2[:, 4 * j:4 * j + 4, :], w_out_dram[:, k0:k0 + 4, :]).then_inc(wout_in[j], 16)
            for name, gone in (("fv", "fq1"), ("rv", "fk1"), ("rg", "rq1")):
                sp.wait_ge(psum_full, full(gone))
                load_chunk(name)

            def one_round(r):
                with sp.Fori(0, EXPERTS) as e:
                    i = r * EXPERTS + e
                    for k in range(KC):
                        sp.wait_ge(w1_used, KC * i + k + 1)
                        sp.dma_start(w1[:, k, :], w_exp_in[0, e, k * P:(k + 1) * P, :]).then_inc(w1_in[k], 16)
                    for k in range(KC):
                        if k < KC - 1:
                            sp.wait_ge(w2_used, (KC - 1) * i + k + 1)
                        else:
                            sp.wait_ge(psum_full, full("out3"))
                            sp.wait_ge(y_done, i + 1)
                        sp.dma_start(w2[:, k, :], w_exp_out[0, e, k * P:(k + 1) * P, :]).then_inc(w2_in[k], 16)
                for t in range(TT):
                    sp.wait_ge(final_ready, TT * r + t + 1)
                    sp.dma_start(out_dram[:, t, :], result[:, t, :]).then_inc(stored, 16)
                sp.wait_ge(stored, 16 * TT * r + 16 * TT)
                sp.sem_inc(round_stored, 1)

            rounds(sp, one_round)

        @block.gpsimd
        def _(pool):
            nc.gpsimd.memset(augq[0:6, :, :], 1.0).then_inc(aug_zero, 1)
            nc.gpsimd.memset(augk[0:6, :, :], 1.0).then_inc(aug_zero, 1)
            pool.wait_ge(const_in, 16)
            for half, whole in ((ident_h, ident), (causal_h, causal), (before_h, before), (ones_h, ones)):
                nc.gpsimd.tensor_copy(half[:, :], whole).then_inc(halves_ready, 1)
            pool.wait_ge(aug_zero, 2)
            pool.wait_ge(gate_f, 1)
            for s in range(3):
                pool.dma_start(augq[3 + s:4 + s, :, :], z_parts[:, s, :]).then_inc(aug_in, 16)
            pool.wait_ge(neg_f, 1)
            for s in range(3):
                pool.dma_start(augk[s:s + 1, :, :], z_parts[:, 3 + s, :]).then_inc(aug_in, 16)
            pool.wait_ge(psum_full, full("qk5"))
            for s in range(3):
                rows = bias[s * EXPERTS:(s + 1) * EXPERTS, :]
                pool.dma_start(rows[:, 0:2 * DM], b_exp_in[0]).then_inc(bias_in, 16)
                pool.dma_start(rows[:, 2 * DM:3 * DM], b_exp_out[0]).then_inc(bias_in, 16)
            n = 3 * EXPERTS
            pool.wait_ge(bias_in, 16 * 6)
            pool.wait_ge(psum_full, full("rs3"))
            nc.gpsimd.tensor_copy(bias_part[0:n, :], bias[0:n, :]).then_inc(pool_done, 1)
            pool.wait_ge(pool_done, 1)
            nc.gpsimd.tensor_tensor(bias_rest[0:n, :], bias[0:n, :], bias_part[0:n, :], ALU.subtract).then_inc(pool_done, 1)
            pool.wait_ge(psum_full, full("rg1"))
            pool.dma_start(area("g_ffn"), norm_ffn_g[0:1, :].to_broadcast([P, DM])).then_inc(gains_in, 16)
            pool.dma_start(area("g_final"), norm_final_g.rearrange("(a d) -> a d", a=1).to_broadcast([P, DM])) \
                .then_inc(gains_in, 16)
            pool.wait_ge(psum_full, full("pv1"))
            pool.wait_ge(pool_done, 2)
            nc.gpsimd.memset(y, 0.0).then_inc(pool_done, 1)
            pool.wait_ge(pool_done, 3)
            nc.gpsimd.tensor_copy(bias_rows[0:EXPERTS, :], bias_part[0:EXPERTS, :]).then_inc(pool_done, 1)
            pool.wait_ge(pool_done, 4)
            nc.gpsimd.tensor_copy(bias_part[0:n, :], bias_rest[0:n, :]).then_inc(pool_done, 1)
            pool.wait_ge(pool_done, 5)
            nc.gpsimd.tensor_copy(bias_rows[EXPERTS:2 * EXPERTS, :], bias_part[EXPERTS:2 * EXPERTS, :]).then_inc(rows_ready, 1)
            nc.gpsimd.tensor_tensor(bias_rows[2 * EXPERTS:n, :], bias_rest[2 * EXPERTS:n, :],
                                    bias_part[2 * EXPERTS:n, :], ALU.subtract).then_inc(rows_ready, 1)

        @block.tensor
        def _(pe):
            mm = nc.tensor.matmul
            for first in (cT_done, rows_used, y_done):
                pe.sem_inc(first, 1)

            def transposes(name, pieces):
                for j, piece in enumerate(pieces):
                    ins = nc.tensor.transpose(bank(name)[:, j * P:(j + 1) * P], piece, ident)
                ins.then_inc(psum_full, 1)

            def project(name):
                pe.wait_ge(chunk_in[name], 16)
                for t in range(TT):
                    free_bank(pe, f"{name}{t}")
                    for k in range(KC):
                        ins = mm(bank(f"{name}{t}"), uT[:, k, t * P:(t + 1) * P], chunk_ap(name)[:, k, :],
                                 start=(k == 0), stop=(k == KC - 1))
                    ins.then_inc(psum_full, 1)

            pe.wait_ge(const_in, 16)
            pe.wait_ge(gain_in, 16)
            nc.tensor.transpose(bank("gT")[:, 0:KC], g_rows[:, :], ident[0:KC, 0:KC]).then_inc(psum_full, 1)
            pe.wait_ge(xn_ready, TT)
            for g in range(4):
                transposes(f"uT{g}", [xn[:, t, k * P:(k + 1) * P] for k in (2 * g, 2 * g + 1) for t in range(TT)])
            pe.wait_ge(freed["act"], drained("uT2"))
            pe.wait_ge(freed["dve"], drained("uT3"))
            project("fq")

            pe.wait_ge(small_in, 16 * 4)
            for k in range(KC):
                ins = mm(bank("fz")[0:FOX_HEADS, 0:SEQ], w_z[:, k, :], uT[:, k, :], start=(k == 0), stop=(k == KC - 1))
            ins.then_inc(psum_full, 1)

            project("fk")
            pe.wait_ge(freed["act"], drained("fq1"))
            for t in range(TT):
                free_bank(pe, f"fqT{t}")
                transposes(f"fqT{t}", [fq[:, t, j * P:(j + 1) * P] for j in range(4)])
            project("rq")
            pe.wait_ge(freed["act"], drained("fk1"))
            for t in range(TT):
                free_bank(pe, f"fkT{t}")
                transposes(f"fkT{t}", [fk[:, t, j * P:(j + 1) * P] for j in range(4)])
            project("rk")

            pe.wait_ge(freed["dve"], drained("fqT1"))
            pe.wait_ge(freed["act"], drained("fkT1"))
            pe.wait_ge(fkz, 2)
            pe.wait_ge(aug_in, 16 * 6)
            pe.wait_ge(halves_ready, 2)
            for g, (t, h0, nh, keys) in enumerate(QK_GROUPS):
                free_bank(pe, f"qk{g}")
                tile = bank(f"qk{g}").rearrange("p (h s) -> p h s", h=nh)
                for j in range(nh):
                    h = h0 + j
                    kT = fkTo if h % 2 else fkTe
                    q = slice(t * P, (t + 1) * P)
                    mm(tile[:, j, :], fqT[:, h // 2, q], kT[:, h // 2, 0:keys], start=True, stop=False)
                    mm(tile[:, j, q], ident_h[:, :], causal_h[:, :], start=False, stop=False, skip_group_check=True)
                    ins = mm(tile[:, j, :], augq[0:6, h, q], augk[0:6, h, 0:keys], start=False, stop=True)
                ins.then_inc(psum_full, 1)

            project("fv")
            for name, src in (("rqT", rq), ("rkT", rk)):
                pe.wait_ge(dve_done, DVE_ROTATED)
                for t in range(TT):
                    free_bank(pe, f"{name}{t}")
                    transposes(f"{name}{t}", [src[:, t, h * P:(h + 1) * P] for h in range(RET_HEADS)])
            project("rv")
            pe.wait_ge(psum_full, full("fv1"))
            pe.sem_inc(w1_used, 2)
            for g, (t, s, h0) in enumerate(PT_GROUPS):
                pe.wait_ge(p_norm, 2 if t == 0 else 6)
                free_bank(pe, f"pT{g}")
                base, width = (0, P) if t == 0 else (TT * NW, SEQ)
                transposes(f"pT{g}", [p_w[:, base + h * width + s * P:base + h * width + s * P + P]
                                      for h in range(h0, h0 + 4)])

            pe.wait_ge(freed["dve"], drained("rqT1"))
            pe.wait_ge(freed["act"], drained("rkT1"))
            for h in range(RET_HEADS):
                free_bank(pe, f"rs{h}")
                mm(bank(f"rs{h}")[:, 0:SEQ], rkT[:, h, 0:P], rqT[:, h, :], start=True, stop=True)
                mm(bank(f"rs{h}")[:, SEQ:384], rkT[:, h, P:SEQ], rqT[:, h, P:SEQ], start=True, stop=True) \
                    .then_inc(psum_full, 1)
            pe.wait_ge(psum_full, full("rv1"))
            pe.sem_inc(w1_used, 2)
            project("rg")

            pe.wait_ge(freed["act"], drained("pT4"))
            pe.wait_ge(freed["dve"], drained("pT5"))
            for g in range(2):
                free_bank(pe, f"pv{g}")
                tile = bank(f"pv{g}").rearrange("p (j t) -> p j t", j=2)
                for jj in range(2):
                    for half in range(2):
                        h = 2 * (2 * g + jj) + half
                        rows = slice(half * FOX_D, (half + 1) * FOX_D)
                        v = slice(h * FOX_D, (h + 1) * FOX_D)
                        mm(tile[rows, jj, :], fv[:, 0, v], pT0[:, h, :], start=True, stop=True)
                        ins = mm(tile[rows, jj, P:SEQ], fv[:, 1, v], pT1[:, h, :], start=False, stop=True,
                                 skip_group_check=True)
                ins.then_inc(psum_full, 1)

            pe.wait_ge(psum_full, full("rg1"))
            pe.sem_inc(w1_used, 4)

            pe.wait_ge(freed["dve"], drained("rs3"))
            pe.wait_ge(freed["act"], drained("rv1"))
            for t in range(TT):
                free_bank(pe, f"ro{t}")
                for h in range(RET_HEADS):
                    d = slice(h * P, (h + 1) * P)
                    o = bank(f"ro{t}")[:, d]
                    if t == 0:
                        ins = mm(o, rsc[:, h, 0:P], rv[:, 0, d], start=True, stop=True)
                    else:
                        mm(o, rsc[:, h, P:SEQ], rv[:, 0, d], start=True, stop=False)
                        ins = mm(o, rsc[:, h, SEQ:384], rv[:, 1, d], start=False, stop=True)
                ins.then_inc(psum_full, 1)

            def out_chunk(j, t):
                for n in range(2):
                    ins = mm(bank(f"out{2 * t + n}"), mixT[:, OUT_ORDER[j], t * P:(t + 1) * P],
                             w2[:, j, n * NW:(n + 1) * NW], start=(j == 0), stop=(j == KC - 1))
                    if j == KC - 1:
                        ins.then_inc(psum_full, 1)
                return ins

            for g in range(4):
                free_bank(pe, f"out{g}")
            pe.wait_ge(freed["act"], drained("pv1"))
            pe.wait_ge(wout_in[0], 16)
            for j in range(4):
                out_chunk(j, 0)
                out_chunk(j, 1).then_inc(w2_used, 1)
            for t in range(TT):
                pe.wait_ge(ron_ready, t + 1)
                free_bank(pe, f"rT{t}")
                transposes(f"rT{t}", [on[:, t, h * P:(h + 1) * P] for h in range(RET_HEADS)])
            pe.wait_ge(freed["act"], drained("rT1"))
            pe.wait_ge(wout_in[1], 16)
            for j in range(4, KC):
                out_chunk(j, 0)
            for j in range(4, KC):
                ins = out_chunk(j, 1)
                if j < KC - 1:
                    ins.then_inc(w2_used, 1)

            for t in range(TT):
                pe.wait_ge(u_ready, t + 1)
                for g in range(2):
                    free_bank(pe, f"vT{t}{g}")
                    transposes(f"vT{t}{g}", [u[:, t, k * P:(k + 1) * P] for k in range(4 * g, 4 * g + 4)])
                free_bank(pe, f"logits{t}")
                for k in range(KC):
                    if k % 4 == 0:
                        name = f"vT{t}{k // 4}"
                        pe.wait_ge(freed[GROUPS[GROUP_AT[name]][1]], drained(name))
                    ins = mm(bank(f"logits{t}")[:, 0:EXPERTS], vT[:, k, t * P:(t + 1) * P],
                             w_rt[:, k, :], start=(k == 0), stop=(k == KC - 1))
                ins.then_inc(psum_full, 1)
            pe.wait_ge(halves_ready, 4)
            pe.wait_ge(picked_ready, 2)
            free_bank(pe, "pos")
            pos = bank("pos")
            mm(pos[:, 0:32], before_h[:, :], picked[:, 0, :], start=True, stop=True)
            mm(pos[:, 32:64], ones_h[:, :], picked[:, 0, :], start=True, stop=False)
            mm(pos[:, 32:64], before_h[:, :], picked[:, 1, :], start=False, stop=True)
            mm(pos[:, 64:96], ones_h[:, :], picked[:, 0, :], start=True, stop=False)
            mm(pos[:, 64:96], ones_h[:, :], picked[:, 1, :], start=False, stop=True).then_inc(psum_full, 1)

            def gather():
                for k in range(KC):
                    n = 0
                    for s in range(3):
                        for t in range(TT):
                            ins = mm(psum[:, XT, k * SLOTS:(k + 1) * SLOTS], u_parts[:, s, t, k * P:(k + 1) * P],
                                     sel[:, t, :], start=(n == 0), stop=(n == 5))
                            n += 1
                ins.then_inc(gath_done, 1)

            def combine(t):
                for half in range(2):
                    ins = mm(psum[:, CB + half, :], cab[:, 2 * half + t, :], y, start=True, stop=True)
                ins.then_inc(comb_done, 1)

            def one_round(r):
                g0 = r * (EXPERTS + 1)
                pe.wait_ge(sel_ready, g0 + 1)
                gather()
                pe.wait_ge(routed, 1)
                pe.wait_ge(rows_ready, 2)
                with pe.Fori(0, EXPERTS) as e:
                    i = r * EXPERTS + e
                    g = r * (EXPERTS + 1) + e
                    pe.wait_ge(xT_ready, g + 1)
                    pe.wait_ge(lc_ready, i + 1)
                    for k in range(KC):
                        pe.wait_ge(w1_in[k], 16 * i + 16)
                        for n in range(2):
                            for half in range(2):
                                cols = slice((2 * n + half) * NW, (2 * n + half + 1) * NW)
                                ins = mm(psum[half * 64:half * 64 + 64, H0 + n, :], xT[:, k, :], w1[:, k, cols],
                                         start=(k == 0), stop=False)
                        ins.then_inc(w1_used, 1)
                        if k == KC // 2:
                            pe.wait_ge(y_ready, i + 1)
                            pe.wait_ge(cab_ready, i + r + 1)
                            pe.wait_ge(comb_added, 2 * g + 1)
                            combine(0)
                    pe.wait_ge(row_ready, i + 1)
                    for n in range(2):
                        for half in range(2):
                            cols = slice((2 * n + half) * NW, (2 * n + half + 1) * NW)
                            ins = mm(psum[half * 64:half * 64 + 64, H0 + n, :], sel_row[:, :],
                                     bias_rows[0:3 * EXPERTS, cols], start=False, stop=True)
                    ins.then_inc(h_ready, 1)

                    pe.wait_ge(sel_ready, g + 2)
                    gather()
                    pe.wait_ge(gs_ready, i + 1)
                    for j in range(4):
                        ins = nc.tensor.transpose(psum[:, CT, j * P:(j + 1) * P],
                                                  gs[:, j % 2, (j // 2) * P:(j // 2 + 1) * P], ident)
                    ins.then_inc(cT_done, 1)
                    pe.wait_ge(a_ready, i + 1)
                    for j in range(4):
                        ins = nc.tensor.transpose(psum[:, AT, j * P:(j + 1) * P], act[:, j * P:(j + 1) * P], ident)
                    ins.then_inc(aT_done, 1)
                    pe.wait_ge(comb_added, 2 * g + 2)
                    combine(1)

                    for half in range(2):
                        ins = mm(psum[half * 64:half * 64 + 64, Y, :], sel_row[:, :],
                                 bias_rows[0:3 * EXPERTS, 2 * DM + half * NW:2 * DM + (half + 1) * NW],
                                 start=True, stop=False)
                    ins.then_inc(rows_used, 1)
                    pe.wait_ge(actT_ready, i + 1)
                    for k in range(KC):
                        pe.wait_ge(w2_in[k], 16 * i + 16)
                        for half in range(2):
                            lhs = actT[:, k % 4, (k // 4) * SLOTS:(k // 4 + 1) * SLOTS]
                            ins = mm(psum[half * 64:half * 64 + 64, Y, :], lhs, w2[:, k, half * NW:(half + 1) * NW],
                                     start=False, stop=(k == KC - 1))
                        if k < KC - 1:
                            ins.then_inc(w2_used, 1)
                    ins.then_inc(y_done, 1)
                pe.wait_ge(y_ready, (r + 1) * EXPERTS + 1)
                pe.wait_ge(cab_ready, (r + 1) * EXPERTS + r + 1)
                pe.wait_ge(comb_added, 2 * (g0 + EXPERTS) + 1)
                combine(0)
                pe.wait_ge(comb_added, 2 * (g0 + EXPERTS) + 2)
                combine(1)

            rounds(pe, one_round)

        @block.scalar
        def _(eng):
            eng.sem_inc(y_ready, 1)
            eng.dma_start(g_rows[:, :], norm_mix_g[0].rearrange("(k p) -> k p", p=P)).then_inc(gain_in, 16)
            eng.dma_start(const[:, 0:4 * P], table[:, 0:4 * P]).then_inc(const_in, 16)
            eng.dma_start(w_z[:, :, :], w_in_dram[:, :, FZ_COL:FZ_COL + FOX_HEADS]).then_inc(small_in, 16)
            with nc.allow_non_contiguous_dma(reason="eight words"):
                eng.dma_start(b_fox[:, :], b_forget[0].rearrange("(p a) -> p a", a=1)).then_inc(small_in, 16)
            eng.dma_start(w_rt[:, :, :], w_router[0].rearrange("(k p) e -> p k e", p=P)).then_inc(small_in, 16)
            eng.dma_start(b_rt[:, :], b_router[0:1, :].to_broadcast([P, EXPERTS])).then_inc(small_in, 16)
            eng.dma_start(const[:, 4 * P:], table[:, 4 * P:]).then_inc(tables_in, 16)

            act_i = nc.scalar.activation

            def copy(o, i, scale=1.0):
                return act_i(o, i, ACT.Copy, scale=scale)

            eng.wait_ge(x_in[0], 16)
            act_i(xn[:, 0, :], acc[:, 0, :], ACT.Square, accum_out=ss[:, 0:1]).then_inc(sq_done, 1)

            def square_roots(event):
                cols = ROOT_COLS[event]
                eng.wait_ge(root_ready, event + 1)
                act_i(root_sqrt[:, cols], root_of[:, cols], ACT.Sqrt).then_inc(seed_ready, 1)

            square_roots(0)

            def scaled_uT(name, g):
                eng.wait_ge(psum_full, full(name))
                for j in range(2):
                    k = 2 * g + j
                    ins = copy(uT[:, k, :], bank(name)[:, j * SEQ:(j + 1) * SEQ], scale=g_mix[:, k:k + 1])
                ins.then_inc(freed["act"], 1)

            def read(name, o, i, scale=1.0):
                eng.wait_ge(psum_full, full(name))
                copy(o, i, scale).then_inc(freed["act"], 1)

            def four(name):
                return bank(name).rearrange("p (j t) -> p j t", j=4)

            eng.wait_ge(psum_full, full("gT"))
            copy(g_mix[:, :], bank("gT")[:, 0:KC]).then_inc(freed["act"], 1)
            eng.wait_ge(freed["act"], drained("gT"))
            scaled_uT("uT0", 0)
            scaled_uT("uT2", 2)
            for t in range(TT):
                read(f"fq{t}", fq[:, t, :], bank(f"fq{t}"), scale=FOX_D ** -0.5)
            z_neg, z_exp, z_log = zwork[0:FOX_HEADS, 1, :], zwork[0:FOX_HEADS, 2, :], zwork[0:FOX_HEADS, 3, :]
            eng.wait_ge(z_abs, 1)
            act_i(z_exp, z_neg, ACT.Exp).then_inc(act_done, 1)
            eng.wait_ge(act_done, 1)
            act_i(z_log, z_exp, ACT.Ln, bias=1.0).then_inc(z_ln, 1)
            for t in range(TT):
                read(f"fk{t}", fk[:, t, :], bank(f"fk{t}"))
            for t in range(TT):
                eng.wait_ge(psum_full, full(f"fkT{t}"))
                cols = slice(t * P, (t + 1) * P)
                copy(fkTe[0:FOX_D, :, cols], four(f"fkT{t}")[0:FOX_D, :, :])
                copy(fkTo[FOX_D:P, :, cols], four(f"fkT{t}")[FOX_D:P, :, :]).then_inc(freed["act"], 1)
            for g, (t, h0, nh, keys) in enumerate(QK_GROUPS):
                eng.wait_ge(max_ready, g + 1)
                base = 0 if t == 0 else TT * NW
                for j in range(nh):
                    h, col = h0 + j, t * FOX_HEADS + h0 + j
                    ins = act_i(p_w[:, base + h * keys:base + (h + 1) * keys], bank(f"qk{g}")[:, j * keys:(j + 1) * keys],
                                ACT.Exp, bias=negmax[:, col:col + 1], accum_out=psum_p[:, col:col + 1])
                ins.then_inc(freed["act"], 1)
            for t in range(TT):
                read(f"fv{t}", fv[:, t, :], bank(f"fv{t}"))
            for t in range(TT):
                read(f"rkT{t}", rkT[:, :, t * P:(t + 1) * P], four(f"rkT{t}"))
            for t in range(TT):
                read(f"rv{t}", rv[:, t, :], bank(f"rv{t}"))

            def read_pT(g):
                t, s, h0 = PT_GROUPS[g]
                dst = pT1[:, h0:h0 + 4, :] if s else pT0[:, h0:h0 + 4, t * P:(t + 1) * P]
                read(f"pT{g}", dst, four(f"pT{g}"))

            for g in (0, 2, 4):
                read_pT(g)
            for t in range(TT):
                eng.wait_ge(psum_full, full(f"rg{t}"))
                act_i(eg[:, t, :], bank(f"rg{t}"), ACT.Exp, scale=-1.0)
                copy(rg[:, t, :], bank(f"rg{t}")).then_inc(freed["act"], 1)
            for g in range(2):
                read(f"pv{g}", mixT[:, 4 + 2 * g:6 + 2 * g, :], bank(f"pv{g}").rearrange("p (j t) -> p j t", j=2))
            for t in range(TT):
                square_roots(1 + t)
            for t in range(TT):
                read(f"rT{t}", mixT[:, 0:RET_HEADS, t * P:(t + 1) * P], four(f"rT{t}"))
            for t in range(TT):
                eng.wait_ge(h_done, t + 1)
                act_i(area("u", TT, DM)[:, t, :], acc[:, t, :], ACT.Square,
                      accum_out=ss[:, TT + t:TT + t + 1]).then_inc(sq_done, 1)
                square_roots(3 + t)
            for name in ("vT00", "vT01", "vT10"):
                t, g = int(name[2]), int(name[3])
                read(name, vT[:, 4 * g:4 * g + 4, t * P:(t + 1) * P], four(name))
            for t in range(TT):
                eng.wait_ge(topv_ready, t + 1)
                act_i(gate4[:, t, :], top_v[:, t, 0:TOP_K], ACT.Exp, bias=negtop[:, t:t + 1],
                      accum_out=gsum[:, t:t + 1]).then_inc(gexp_ready, 1)

            def read_xT():
                copy(xT[:, :, :], psum[:, XT, :].rearrange("p (k s) -> p k s", k=KC)).then_inc(xT_ready, 1)

            def one_round(r):
                g0 = r * (EXPERTS + 1)
                eng.wait_ge(gath_done, g0 + 1)
                read_xT()
                with eng.Fori(0, EXPERTS) as e:
                    i = r * EXPERTS + e
                    g = r * (EXPERTS + 1) + e
                    eng.wait_ge(gm_ready, i + 1)
                    act_i(sg, gm, ACT.Sigmoid, scale=ALPHA).then_inc(sg_ready, 1)
                    eng.wait_ge(gath_done, g + 2)
                    read_xT()
                    eng.wait_ge(aT_done, i + 1)
                    copy(actT[:, :, :], psum[:, AT, :].rearrange("p (j q) -> p j q", j=4)).then_inc(actT_ready, 1)
                    eng.wait_ge(cT_done, i + 2)
                    eng.wait_ge(comb_done, 2 * g + 2)
                    copy(cab[:, :, :], psum[:, CT, :].rearrange("p (j q) -> p j q", j=4)).then_inc(cab_ready, 1)
                    eng.wait_ge(y_done, i + 2)
                    copy(y, psum[:, Y, :]).then_inc(y_ready, 1)
                eng.wait_ge(comb_added, 2 * (g0 + EXPERTS) + 2)
                act_i(result[:, 0, :], acc[:, 0, :], ACT.Square, accum_out=ss[:, 0:1]).then_inc(final_sq, 1)
                eng.wait_ge(final_w, r + 1)
                act_i(root_sqrt[:, ROOT_COLS[5]], root_of[:, ROOT_COLS[5]], ACT.Sqrt).then_inc(final_seed, 1)

            rounds(eng, one_round)

        @block.vector
        def _(dve):
            v = nc.vector
            steps = [0]
            for first in (lc_ready, comb_added):
                dve.sem_inc(first, 1)

            def then(ins):
                steps[0] += 1
                ins.then_inc(dve_done, 1)
                dve.wait_ge(dve_done, steps[0])

            def inverse_roots(event, square, scale, eps):
                cols = ROOT_COLS[event]
                w, r, t = root_of[:, cols], inv_root[:, cols], root_t[:, cols]
                if event:
                    dve.wait_ge(root_ready, event)
                v.tensor_scalar(w, square, scale, eps, ALU.mult, ALU.add).then_inc(root_ready, 1)
                dve.wait_ge(seed_ready, event + 1)
                then(v.reciprocal(r, root_sqrt[:, cols]))
                then(v.tensor_tensor(t, r, r, ALU.mult))
                then(v.tensor_tensor(t, t, w, ALU.mult))
                then(v.tensor_scalar(t, t, -0.5, 1.5, ALU.mult, ALU.add))
                then(v.tensor_tensor(r, r, t, ALU.mult))

            v.memset(fkTe[FOX_D:P, :, :], 0.0).then_inc(fkz, 1)
            v.memset(fkTo[0:FOX_D, :, :], 0.0).then_inc(fkz, 1)
            then(v.memset(slot_of[:, :, :], -UNPICKED))
            dve.wait_ge(x_in[1], 16)
            then(v.tensor_tensor_reduce(xn[:, 1, :], acc[:, 1, :], acc[:, 1, :], 1.0, 0.0, ALU.mult, ALU.add, ss[:, 1:2]))
            dve.wait_ge(sq_done, 1)
            inverse_roots(0, ss[:, 0:TT], 1.0 / DM, RMS_EPS)
            for t in range(TT):
                v.tensor_scalar(xn[:, t, :], acc[:, t, :], inv_root[:, t:t + 1], None, ALU.mult).then_inc(xn_ready, 1)

            dve.wait_ge(freed["act"], drained("gT"))
            for name, g in (("uT1", 1), ("uT3", 3)):
                dve.wait_ge(psum_full, full(name))
                for j in range(2):
                    k = 2 * g + j
                    ins = v.tensor_scalar(uT[:, k, :], bank(name)[:, j * SEQ:(j + 1) * SEQ], g_mix[:, k:k + 1],
                                          None, ALU.mult)
                ins.then_inc(freed["dve"], 1)

            zb, zneg, zlog, zls, zf, znf = (zwork[0:FOX_HEADS, j, :] for j in (0, 1, 3, 4, 5, 6))
            dve.wait_ge(small_in, 16 * 4)
            dve.wait_ge(psum_full, full("fz"))
            v.tensor_scalar(zb, bank("fz")[0:FOX_HEADS, 0:SEQ], b_fox[:, 0:1], None, ALU.add).then_inc(freed["dve"], 1)
            dve.wait_ge(freed["dve"], drained("fz"))
            v.scalar_tensor_tensor(out=zneg, in0=zb, scalar=-1.0, in1=zb, op0=ALU.mult, op1=ALU.min).then_inc(z_abs, 1)
            dve.wait_ge(z_ln, 1)
            then(v.scalar_tensor_tensor(out=zls, in0=zb, scalar=0.0, in1=zlog, op0=ALU.min, op1=ALU.subtract))
            dve.wait_ge(const_in, 16)
            then(v.tensor_tensor_scan(zf, const[0:FOX_HEADS, CONST_AT["ones"][0]:CONST_AT["ones"][0] + 1].to_broadcast([FOX_HEADS, SEQ]),
                                      zls, 0.0, ALU.mult, ALU.add))
            then(v.tensor_copy(z_parts[:, 0, :], zf))
            then(v.tensor_tensor(znf, zf, z_parts[:, 0, :], ALU.subtract))
            then(v.tensor_copy(z_parts[:, 1, :], znf))
            v.tensor_tensor(z_parts[:, 2, :], znf, z_parts[:, 1, :], ALU.subtract).then_inc(gate_f, 1)
            dve.wait_ge(gate_f, 1)
            v.tensor_scalar(z_parts[:, 3:6, :], z_parts[:, 0:3, :], -1.0, None, ALU.mult).then_inc(neg_f, 1)

            def four(name):
                return bank(name).rearrange("p (j t) -> p j t", j=4)

            def read(name, o, i):
                dve.wait_ge(psum_full, full(name))
                v.tensor_copy(o, i).then_inc(freed["dve"], 1)

            for t in range(TT):
                read(f"fqT{t}", fqT[:, :, t * P:(t + 1) * P], four(f"fqT{t}"))

            def rotate(name, dst, t):
                dve.wait_ge(psum_full, full(name))
                src = bank(name).rearrange("p (h a j) -> p h a j", h=RET_HEADS, a=2)
                part = rot[:, 0, :].rearrange("p (h a j) -> p h a j", h=RET_HEADS, a=2)
                turn = rot[:, 1, :].rearrange("p (h a j) -> p h a j", h=RET_HEADS, a=2)
                shape = [P, RET_HEADS, 64]
                for a in range(2):
                    v.tensor_tensor(part[:, :, a, :], src[:, :, a, :], cos[:, t:t + 1, :].to_broadcast(shape), ALU.mult)
                v.tensor_tensor(turn[:, :, 0, :], src[:, :, 1, :], negsin[:, t:t + 1, :].to_broadcast(shape), ALU.mult)
                v.tensor_tensor(turn[:, :, 1, :], src[:, :, 0, :], sin[:, t:t + 1, :].to_broadcast(shape), ALU.mult) \
                    .then_inc(freed["dve"], 1)
                dve.wait_ge(freed["dve"], drained(name))
                then(v.tensor_tensor(dst[:, t, :], rot[:, 0, :], rot[:, 1, :], ALU.add))

            dve.wait_ge(tables_in, 16)
            for name, dst in (("rq", rq), ("rk", rk)):
                for t in range(TT):
                    rotate(f"{name}{t}", dst, t)
            assert steps[0] == DVE_ROTATED

            for g, (t, h0, nh, keys) in enumerate(QK_GROUPS):
                dve.wait_ge(psum_full, full(f"qk{g}"))
                col = t * FOX_HEADS + h0
                v.tensor_reduce(negmax[:, col:col + nh], bank(f"qk{g}").rearrange("p (h s) -> p h s", h=nh),
                                AX.X, ALU.max, negate=True).then_inc(max_ready, 1)
            for g, (t, h0, nh, keys) in enumerate(QK_GROUPS):
                dve.wait_ge(freed["act"], drained(f"qk{g}"))
                col = t * FOX_HEADS + h0
                base = (0 if t == 0 else TT * NW) + h0 * keys
                tile = p_w[:, base:base + nh * keys].rearrange("p (h s) -> p h s", h=nh)
                then(v.reciprocal(rsum_p[:, col:col + nh], psum_p[:, col:col + nh]))
                scale = rsum_p[:, col:col + nh].rearrange("p (h a) -> p h a", a=1).to_broadcast([P, nh, keys])
                v.tensor_tensor(tile, tile, scale, ALU.mult).then_inc(p_norm, 1)
            for t in range(TT):
                read(f"rqT{t}", rqT[:, :, t * P:(t + 1) * P], four(f"rqT{t}"))
            for g in (1, 3, 5):
                t, s, h0 = PT_GROUPS[g]
                dst = pT1[:, h0:h0 + 4, :] if s else pT0[:, h0:h0 + 4, t * P:(t + 1) * P]
                read(f"pT{g}", dst, four(f"pT{g}"))
            for h in range(RET_HEADS):
                dve.wait_ge(psum_full, full(f"rs{h}"))
                v.tensor_tensor(rsc[:, h, :], bank(f"rs{h}")[:, 0:384], decay[:, h, :], ALU.mult) \
                    .then_inc(freed["dve"], 1)
            dve.wait_ge(freed["act"], drained("rg1"))
            then(v.tensor_scalar(area("eg"), area("eg"), 1.0, None, ALU.add))
            then(v.reciprocal(area("eg"), area("eg")))
            then(v.tensor_tensor(area("rg"), area("rg"), area("eg"), ALU.mult))
            for t in range(TT):
                dve.wait_ge(psum_full, full(f"ro{t}"))
                tile = bank(f"ro{t}").rearrange("p (h d) -> p h d", h=RET_HEADS)
                for h in range(RET_HEADS):
                    ins = v.bn_stats(stats[:, h, :], tile[:, h, :])
                then(ins)
                for h in range(RET_HEADS):
                    ins = v.bn_aggr(mv[:, h, :], stats[:, h, :])
                then(ins)
                inverse_roots(1 + t, mv[:, :, 1], 1.0, GN_EPS)
                for h in range(RET_HEADS):
                    ins = v.tensor_scalar(on[:, t, h * P:(h + 1) * P], tile[:, h, :], mv[:, h, 0:1],
                                          inv_root[:, ROOT_COLS[1 + t].start + h:ROOT_COLS[1 + t].start + h + 1], ALU.subtract, ALU.mult)
                ins.then_inc(freed["dve"], 1)
                dve.wait_ge(freed["dve"], drained(f"ro{t}"))
                v.tensor_tensor(on[:, t, :], on[:, t, :], rg[:, t, :], ALU.mult).then_inc(ron_ready, 1)
            uf, rest = area("u", TT, DM), area("u_rest", TT, DM)

            def add_mix(t):
                for n in range(2):
                    g = 2 * t + n
                    dve.wait_ge(psum_full, full(f"out{g}"))
                    cols = slice(n * NW, (n + 1) * NW)
                    v.tensor_tensor(acc[:, t, cols], acc[:, t, cols], bank(f"out{g}"), ALU.add).then_inc(freed["dve"], 1)
                dve.wait_ge(freed["dve"], drained(f"out{2 * t + 1}"))
                dve.sem_inc(h_done, 1)

            def norm_h(t):
                dve.wait_ge(sq_done, 2 + t)
                inverse_roots(3 + t, ss[:, TT + t:TT + t + 1], 1.0 / DM, RMS_EPS)
                v.scalar_tensor_tensor(out=u[:, t, :], in0=acc[:, t, :], scalar=inv_root[:, ROOT_COLS[3 + t]],
                                       in1=area("g_ffn"), op0=ALU.mult, op1=ALU.mult).then_inc(u_ready, 1)
                dve.wait_ge(u_ready, t + 1)

            def split_u(t, n):
                left = uf[:, t, :] if n == 0 else rest[:, t, :]
                then(v.tensor_copy(u_parts[:, n, t, :], left))
                out_ = rest[:, t, :] if n == 0 else u_parts[:, 2, t, :]
                then(v.tensor_tensor(out_, left, u_parts[:, n, t, :], ALU.subtract))

            def pick(t):
                name = f"logits{t}"
                dve.wait_ge(psum_full, full(name))
                v.tensor_tensor(logits[:, t, :], bank(name)[:, 0:EXPERTS], b_rt[:, :], ALU.add).then_inc(freed["dve"], 1)
                dve.wait_ge(freed["dve"], drained(name))
                then(v.max(top_v[:, t, :], logits[:, t, :]))
                then(v.max_index(top_i[:, t, :], top_v[:, t, :], logits[:, t, :]))
                shape = [P, TOP_K, EXPERTS]
                then(v.tensor_tensor(onehot[:, t, :, :], expert_ids.rearrange("p (a e) -> p a e", a=1).to_broadcast(shape),
                                     top_i[:, t, 0:TOP_K].rearrange("p (j a) -> p j a", a=1).to_broadcast(shape),
                                     ALU.is_equal))
                v.tensor_reduce(picked[:, t, :], onehot[:, t, :, :].rearrange("p j e -> p e j"), AX.X, ALU.max) \
                    .then_inc(picked_ready, 1)
                v.tensor_scalar(negtop[:, t:t + 1], top_v[:, t, 0:1], -1.0, None, ALU.mult).then_inc(topv_ready, 1)

            dve.wait_ge(gains_in, 32)
            add_mix(0)
            norm_h(0)
            dve.wait_ge(rows_ready, 2)
            split_u(0, 0)
            add_mix(1)
            split_u(0, 1)
            norm_h(1)
            split_u(1, 0)
            pick(0)
            read("vT11", vT[:, 4:8, P:SEQ], four("vT11"))
            split_u(1, 1)
            pick(1)
            dve.wait_ge(picked_ready, TT)
            then(v.tensor_scalar(unpicked[:, :, :], picked[:, :, :], UNPICKED, UNPICKED, ALU.mult, ALU.subtract))
            dve.wait_ge(psum_full, full("pos"))
            pos = bank("pos")
            then(v.tensor_tensor(slot_of[:, :, 0:EXPERTS], pos[:, 0:64].rearrange("p (t e) -> p t e", t=TT),
                                 unpicked[:, :, :], ALU.add))

            def count_and_gates():
                v.tensor_reduce(most[0:1, 0:1], pos[0:1, 64:96], AX.X, ALU.max).then_inc(routed, 1)
                dve.wait_ge(gexp_ready, TT)
                then(v.reciprocal(gsum[:, :], gsum[:, :]))
                shape = [P, TOP_K, EXPERTS]
                for t in range(TT):
                    then(v.tensor_scalar(gate4[:, t, :], gate4[:, t, :], gsum[:, t:t + 1], None, ALU.mult))
                    then(v.tensor_tensor(gated[:, t, :, :], onehot[:, t, :, :],
                                         gate4[:, t, :].rearrange("p (j a) -> p j a", a=1).to_broadcast(shape), ALU.mult))
                    then(v.tensor_reduce(gates[:, t, :], gated[:, t, :, :].rearrange("p j e -> p e j"), AX.X, ALU.add))

            def select(e):
                for t in range(TT):
                    ins = v.tensor_scalar(sel[:, t, :], slot_ids[:, 0:SLOTS], slot_of[:, t, bass.ds(e, 1)], None, ALU.is_equal)
                ins.then_inc(sel_ready, 1)

            def add_combined(t):
                v.tensor_tensor(acc[:, t, :], acc[:, t, :], psum[:, CB:CB + 2, :].rearrange("p b n -> p (b n)"),
                                ALU.add).then_inc(comb_added, 1)

            def one_round(r):
                g0 = r * (EXPERTS + 1)
                with dve.If(r > 0):
                    v.tensor_scalar(slot_of[:, :, :], slot_of[:, :, :], float(SLOTS), None, ALU.subtract).then_inc(moved, 1)
                    dve.wait_ge(moved, r)
                    select(0)
                v.memset(cab[:, :, :], 0.0).then_inc(cab_ready, 1)
                with dve.Fori(0, EXPERTS) as e:
                    i = r * EXPERTS + e
                    g = r * (EXPERTS + 1) + e
                    dve.wait_ge(gath_done, g + 1)
                    select(e + 1)
                    dve.wait_ge(cT_done, i + 1)
                    for t in range(TT):
                        ins = v.tensor_scalar(gs[:, t, :], slot_ids, slot_of[:, t, bass.ds(e, 1)],
                                              gates[:, t, bass.ds(e, 1)], ALU.is_equal, ALU.mult)
                    ins.then_inc(gs_ready, 1)
                    dve.wait_ge(rows_used, i + 1)
                    v.tensor_scalar(sel_row[:, :], ones[0:3 * EXPERTS, 0:SLOTS], piece_row[0:3 * EXPERTS, bass.ds(e, 1)],
                                    None, ALU.mult).then_inc(row_ready, 1)
                    dve.wait_ge(h_ready, i + 1)
                    v.tensor_scalar(gm, psum[:, H0, :], LIMIT, None, ALU.min).then_inc(gm_ready, 1)
                    v.tensor_scalar(lc, psum[:, H1, :], LIMIT, -LIMIT, ALU.min, ALU.max).then_inc(lc_ready, 1)
                    dve.wait_ge(lc_ready, i + 2)
                    v.scalar_tensor_tensor(out=lg, in0=lc, scalar=1.0, in1=gm, op0=ALU.add, op1=ALU.mult) \
                        .then_inc(lg_ready, 1)
                    dve.wait_ge(lg_ready, i + 1)
                    dve.wait_ge(sg_ready, i + 1)
                    v.tensor_tensor(act, lg, sg, ALU.mult).then_inc(a_ready, 1)
                    for t in range(TT):
                        dve.wait_ge(comb_done, 2 * g + t + 1)
                        add_combined(t)
                for t in range(TT):
                    dve.wait_ge(comb_done, 2 * (g0 + EXPERTS) + t + 1)
                    add_combined(t)
                cols = ROOT_COLS[5]
                w, root, t_ = root_of[:, cols], inv_root[:, cols], root_t[:, cols]
                dve.wait_ge(comb_added, 2 * (g0 + EXPERTS) + 3)
                v.tensor_tensor_reduce(result[:, 1, :], acc[:, 1, :], acc[:, 1, :], 1.0, 0.0,
                                       ALU.mult, ALU.add, ss[:, 1:2]).then_inc(final_step, 1)
                dve.wait_ge(final_step, 6 * r + 1)
                dve.wait_ge(final_sq, r + 1)
                v.tensor_scalar(w, ss[:, 0:TT], 1.0 / DM, RMS_EPS, ALU.mult, ALU.add).then_inc(final_w, 1)
                dve.wait_ge(final_seed, r + 1)
                v.reciprocal(root, root_sqrt[:, cols]).then_inc(final_step, 1)
                dve.wait_ge(final_step, 6 * r + 2)
                v.tensor_tensor(t_, root, root, ALU.mult).then_inc(final_step, 1)
                dve.wait_ge(final_step, 6 * r + 3)
                v.tensor_tensor(t_, t_, w, ALU.mult).then_inc(final_step, 1)
                dve.wait_ge(final_step, 6 * r + 4)
                v.tensor_scalar(t_, t_, -0.5, 1.5, ALU.mult, ALU.add).then_inc(final_step, 1)
                dve.wait_ge(final_step, 6 * r + 5)
                v.tensor_tensor(root, root, t_, ALU.mult).then_inc(final_step, 1)
                dve.wait_ge(final_step, 6 * r + 6)
                for t in range(TT):
                    col = cols.start + t
                    v.scalar_tensor_tensor(out=result[:, t, :], in0=acc[:, t, :], scalar=inv_root[:, col:col + 1],
                                           in1=area("g_final"), op0=ALU.mult, op1=ALU.mult).then_inc(final_ready, 1)

            select(0)
            count_and_gates()
            rounds(dve, one_round)


DVE_ROTATED = 16

_INS = ["x", "norm_mix_g", "w_in", "b_forget", "w_out", "norm_ffn_g", "w_router", "b_router",
        "w_exp_in", "b_exp_in", "w_exp_out", "b_exp_out", "norm_final_g"]


def kernel(**inputs):
    import numpy as _np
    import concourse.bacc as _bacc
    from concourse import mybir as _mybir
    from concourse.bass_utils import run_bass_kernel_spmd as _run

    nc = _bacc.Bacc("TRN2", target_bir_lowering=False, num_devices=1)
    arrays, args = {}, []
    given = [(name, _np.ascontiguousarray(inputs[name])) for name in _INS] + [("table", constant_table())]
    for name, a in given:
        arrays[f"in_{name}"] = a
        args.append(nc.dram_tensor(f"in_{name}", a.shape, _mybir.dt.from_np(a.dtype), kind="ExternalInput").ap())
    o = nc.dram_tensor("out_0", (1, SEQ, DM), _mybir.dt.float32, kind="ExternalOutput").ap()
    build(nc, *args, o)
    r = _run(nc, [arrays], core_ids=[0])
    return r.results[0]["out_0"]
```

```python
from contextlib import ExitStack

import numpy as np

import concourse.bass as bass
from concourse import mybir

F32 = mybir.dt.float32
BF16 = mybir.dt.bfloat16
I32 = mybir.dt.int32
U32 = mybir.dt.uint32
ALU = mybir.AluOpType
ACT = mybir.ActivationFunctionType
AX = mybir.AxisListType

P = 128
SEQ, DM = 256, 1024
TT = SEQ // P
KC = DM // P
NW = 512
RET_HEADS, RET_D = 4, 128
FOX_HEADS, FOX_D = 8, 64
CHUNK = 64
EXPERTS, TOP_K = 32, 4
SLOTS = 64
ROUNDS = SEQ // SLOTS
UNPICKED = 1024.0
RMS_EPS = GN_EPS = 1e-5
LIMIT, ALPHA = 7.0, 1.702
WAKING = 40
MASKED = -1e30

CONST_COLS = [("ident", P), ("before", P), ("ones", P), ("causal", P), ("cos", TT * 64),
              ("sin", TT * 64), ("negsin", TT * 64), ("decay", RET_HEADS * 384),
              ("slot_ids", 4 * SLOTS), ("expert_ids", EXPERTS), ("piece_row", EXPERTS + 2),
              ("stack", EXPERTS)]
CONST_AT = {}
_n = 0
for _name, _w in CONST_COLS:
    CONST_AT[_name] = (_n, _w)
    _n += _w
CONST_W = _n


def constant_table():
    t = np.zeros((P, CONST_W), np.float32)

    def put(name, a):
        at, w = CONST_AT[name]
        t[:a.shape[0], at:at + w] = a.reshape(a.shape[0], w)

    i = np.arange(P)
    put("ident", np.eye(P, dtype=np.float32))
    put("before", (i[:, None] < i[None, :]).astype(np.float32))
    put("ones", np.ones((P, P), np.float32))
    put("causal", np.where(i[None, :] <= i[:, None], 0.0, MASKED).astype(np.float32))
    half = RET_D // 2
    freq = np.float32(10000.0) ** (-np.arange(half, dtype=np.float32) / np.float32(half))
    angle = (np.arange(SEQ, dtype=np.float32)[:, None] * freq[None, :]).reshape(TT, P, half)
    angle = angle.transpose(1, 0, 2).astype(np.float64)
    put("cos", np.cos(angle).astype(np.float32))
    put("sin", np.sin(angle).astype(np.float32))
    put("negsin", -np.sin(angle).astype(np.float32))
    log_gamma = np.log1p(-np.exp2(-5.0 - np.arange(RET_HEADS)))
    dec = np.zeros((P, RET_HEADS, 384))
    for key0, query0, at, n in ((0, 0, 0, SEQ), (P, P, SEQ, P)):
        s = key0 + i[:, None]
        q = query0 + np.arange(n)[None, :]
        seen = s // CHUNK <= q // CHUNK
        for h in range(RET_HEADS):
            dec[:, h, at:at + n] = np.where(seen, np.exp(log_gamma[h] * np.abs(q - s)), 0.0)
    put("decay", (dec * RET_D ** -0.5).astype(np.float32))
    ids = np.arange(SLOTS)
    none = np.full(SLOTS, 0.5)
    put("slot_ids", np.broadcast_to(np.concatenate([ids, none, none, ids]), (P, 4 * SLOTS)).astype(np.float32))
    put("expert_ids", np.broadcast_to(np.arange(EXPERTS), (P, EXPERTS)).astype(np.float32))
    rows = np.zeros((P, EXPERTS + 2), np.float32)
    rows[:3 * EXPERTS, :EXPERTS] = np.tile(np.eye(EXPERTS), (3, 1))
    put("piece_row", rows)
    put("stack", np.tile(np.eye(EXPERTS), (P // EXPERTS, 1)).astype(np.float32))
    return t


GROUPS = (
    [("gT", "dve"), ("uT00", "act"), ("uT01", "dve"), ("uT10", "act"), ("uT11", "dve")]
    + [("fq0", "act"), ("fq1", "act"), ("rr", "dve"), ("zp", "dve"), ("fk0", "act"), ("fk1", "act"), ("fz", "dve")]
    + [("fqT0", "dve"), ("fqT1", "dve")]
    + [("rq0", "dve"), ("rq1", "dve"), ("fkT0", "act"), ("fkT1", "act")]
    + [("rk0", "dve"), ("rk1", "dve")]
    + [(f"qk{g}", "act") for g in range(6)]
    + [("fv0", "act"), ("fv1", "act")]
    + [("rqT0", "dve"), ("rqT1", "dve"), ("rkT0", "act"), ("rkT1", "act")]
    + [("rv0", "act"), ("rv1", "act")]
    + [(f"pT{g}", "dve" if g % 2 else "act") for g in range(6)]
    + [(f"rs{h}", "dve") for h in range(RET_HEADS)]
    + [("rg0", "act"), ("rg1", "act"), ("pv0", "act"), ("pv1", "act")]
    + [("ro0", "dve"), ("ro1", "dve"), ("rT0", "act"), ("rT1", "act")]
    + [("out0", "dve"), ("out1", "dve"), ("hT00", "act"), ("hT01", "act"), ("part0", "act")]
    + [("out2", "dve"), ("out3", "dve"), ("logits0", "dve")]
    + [("hT10", "act"), ("hT11", "act"), ("part1", "act"), ("logits1", "dve"), ("pos", "dve")]
)
GROUP_AT = {name: n for n, (name, _) in enumerate(GROUPS)}
BANKS = 8
BANK_OF = {name: n % BANKS for name, n in GROUP_AT.items()}
_b = BANK_OF["ro0"]
BANK_OF.update({name: (_b + step) % BANKS for name, step in (
    ("out0", 4), ("out1", 5), ("out2", 6), ("out3", 7), ("hT00", 0), ("hT01", 1), ("part0", 2), ("logits0", 3),
    ("hT10", 0), ("hT11", 1), ("part1", 2), ("logits1", 4), ("pos", 6))})

QK_GROUPS = [(0, 0, 4, P), (0, 4, 4, P)] + [(1, 2 * j, 2, SEQ) for j in range(4)]
PT_GROUPS = [(0, 0, 0), (0, 0, 4), (1, 0, 0), (1, 0, 4), (1, 1, 0), (1, 1, 4)]

CHUNKS = [("fq", 2048, 0), ("fk", 2560, 1), ("rq", 0, 2), ("rk", 512, 3),
          ("fv", 3072, 0), ("rv", 1024, 1), ("rg", 1536, 2)]
FZ_COL = 3584
SLOT_OF = {name: s for name, _, s in CHUNKS}
OUT_ORDER = [4, 5, 6, 7, 0, 1, 2, 3]

ARENA = {
    "uT": (0, 2048), "scratch": (2048, 2048), "diag": (3072, 256), "fq": (4096, 1024), "p": (2048, 3072),
    "fk": (5120, 1024), "rq": (6144, 1024), "rk": (7168, 1024), "pT": (5120, 3072),
    "fqT": (8192, 1024), "fkTe": (9216, 1024), "fkTo": (10240, 1024),
    "fv": (11264, 1024), "zwork": (11264, 1792), "z_parts": (13056, 768),
    "rqT": (12288, 1024), "rkT": (13312, 1024),
    "rv": (14336, 1024), "rg": (15360, 1024), "augq": (14336, 1024), "augk": (15360, 1024),
    "eg": (16384, 1024), "on": (17408, 1024), "zpart": (17408, 256),
    "rot": (18432, 1024), "rsc": (18432, 1536),
    "g_ffn": (0, 1024), "g_final": (1024, 1024),
    "bias": (8192, 3072), "bias_rest": (2048, 3072), "bias_rows": (11264, 1536), "bias_part": (12800, 1536),
    "u": (5120, 2048), "u_rest": (9216, 2048), "u_parts": (16384, 3072), "hT": (14336, 2048),
    "xT": (8192, 512), "gm": (8704, 512), "lc": (9216, 512), "lg": (9728, 512), "sg": (10240, 512),
    "act": (10752, 512), "actT": (4096, 512), "cab": (4608, 512), "gs": (7168, 512), "y": (7680, 512),
    "onehot": (19456, 256), "gated": (19712, 256), "result": (5120, 2048),
}
ARENA_W = 19968
ROOT_COLS = [slice(0, 2), slice(2, 6), slice(6, 10), slice(10, 11), slice(11, 12), slice(12, 14)]
RESULT_PARTS = [(t, slice(n * NW, (n + 1) * NW)) for t in range(TT) for n in range(DM // NW)]
RING_W2 = KC * 2 * DM
RING_W = RING_W2 + KC * DM


def build(nc, x, norm_mix_g, w_in, b_forget, w_out, norm_ffn_g, w_router, b_router,
          w_exp_in, b_exp_in, w_exp_out, b_exp_out, norm_final_g, table, out):
    with ExitStack() as ctx:
        def sb(name, shape, dt=F32):
            return ctx.enter_context(nc.sbuf_tensor(name, shape, dt))

        def sem(name):
            return ctx.enter_context(nc.semaphore(name))

        ring = sb("ring", [P, RING_W])
        arena = sb("arena", [P, ARENA_W])
        const = sb("const", [P, CONST_W])
        acc = sb("acc", [P, TT, DM])
        mixT = sb("mixT", [P, KC, SEQ])
        w_z = sb("w_z", [P, KC, FOX_HEADS])
        g_rows = sb("g_rows", [2 * KC, P])
        g_cols = sb("g_cols", [P, 2 * KC])
        ident_h = sb("ident_h", [P, P], BF16)
        before_h = sb("before_h", [P, P], BF16)
        ones_h = sb("ones_h", [P, P], BF16)
        causal_h = sb("causal_h", [P, P], BF16)
        b_fox = sb("b_fox", [FOX_HEADS, 1])
        w_rt = sb("w_rt", [P, KC, EXPERTS])
        b_rt = sb("b_rt", [P, EXPERTS])
        ss = sb("ss", [P, 2 * TT])
        negmax = sb("negmax", [P, TT * FOX_HEADS])
        psum_p = sb("psum_p", [P, TT * FOX_HEADS])
        rsum_p = sb("rsum_p", [P, TT * FOX_HEADS])
        stats = sb("stats", [P, RET_HEADS, 6])
        mv = sb("mv", [P, RET_HEADS, 2])
        root_eighth = sb("root_eighth", [P, TT])
        minus_root = sb("minus_root", [P, TT])
        root_of = sb("root_of", [P, 14])
        inv_root = sb("inv_root", [P, 14])
        root_t = sb("root_t", [P, 14])
        root_sqrt = sb("root_sqrt", [P, 14])
        partial = sb("partial", [P, TT, P])
        logits = sb("logits", [P, TT, EXPERTS])
        top_v = sb("top_v", [P, TT, 8])
        top_i = sb("top_i", [P, TT, 8], U32)
        gate4 = sb("gate4", [P, TT, TOP_K])
        gsum = sb("gsum", [P, TT])
        negtop = sb("negtop", [P, TT])
        picked = sb("picked", [P, TT, EXPERTS], BF16)
        unpicked = sb("unpicked", [P, TT, EXPERTS])
        gates = sb("gates", [P, TT, EXPERTS])
        slot_of = sb("slot_of", [P, TT, EXPERTS + 2])
        most = sb("most", [1, 1], I32)
        sel = sb("sel", [P, TT, SLOTS], BF16)
        sel_row = sb("sel_row", [3 * EXPERTS, SLOTS], BF16)
        psum = ctx.enter_context(nc.psum_tensor("psum", [P, BANKS, NW], F32))

        def area(name, *shape):
            at, w = ARENA[name]
            v = arena[:, at:at + w]
            if len(shape) == 2:
                v = v.rearrange("p (a b) -> p a b", a=shape[0])
            if len(shape) == 3:
                v = v.rearrange("p (a b c) -> p a b c", a=shape[0], b=shape[1])
            return v

        def c(name):
            at, w = CONST_AT[name]
            return const[:, at:at + w]

        ident, before, ones, causal = c("ident"), c("before"), c("ones"), c("causal")
        cos, sin, negsin = (c(n).rearrange("p (t j) -> p t j", t=TT) for n in ("cos", "sin", "negsin"))
        decay = c("decay").rearrange("p (h j) -> p h j", h=RET_HEADS)
        slot_ids, expert_ids, piece_row, stack = c("slot_ids"), c("expert_ids"), c("piece_row"), c("stack")

        uT = area("uT", KC, SEQ)
        scratch, diag = area("scratch", TT, DM), area("diag", TT, P)
        fq, fk, fv = (area(n, TT, NW) for n in ("fq", "fk", "fv"))
        rq, rk, rv, rg, eg, on = (area(n, TT, NW) for n in ("rq", "rk", "rv", "rg", "eg", "on"))
        fqT, fkTe, fkTo = (area(n, 4, SEQ) for n in ("fqT", "fkTe", "fkTo"))
        rqT, rkT = (area(n, RET_HEADS, SEQ) for n in ("rqT", "rkT"))
        rot = area("rot", 2, NW)
        rsc = area("rsc", RET_HEADS, 384)
        augq, augk = (area(n).bitcast(BF16).rearrange("p (h t) -> p h t", h=FOX_HEADS) for n in ("augq", "augk"))
        zwork = area("zwork", 7, SEQ)
        z_parts = area("z_parts").bitcast(BF16)[0:FOX_HEADS, :].rearrange("p (s t) -> p s t", s=6)
        onehot, gated = (area(n).rearrange("p (t j e) -> p t j e", t=TT, j=TOP_K) for n in ("onehot", "gated"))
        zpart = area("zpart")
        p_w, pT_w = area("p"), area("pT")
        pT0 = pT_w[:, 0:2048].rearrange("p (h t) -> p h t", h=FOX_HEADS)
        pT1 = pT_w[:, 2048:3072].rearrange("p (h t) -> p h t", h=FOX_HEADS)
        hT = area("hT", KC, SEQ)
        u = area("u", TT, DM)
        u_rest = area("u_rest", TT, DM)
        u_parts = area("u_parts").bitcast(BF16).rearrange("p (s t d) -> p s t d", s=3, t=TT)
        bias, bias_rest = area("bias"), area("bias_rest")
        bias_rows, bias_part = area("bias_rows").bitcast(BF16), area("bias_part").bitcast(BF16)
        xT = area("xT", KC, SLOTS)
        gm, lc, lg, sg, act, y = (area(n) for n in ("gm", "lc", "lg", "sg", "act", "y"))
        actT, cab = area("actT", 4, P), area("cab", 4, P)
        gs = area("gs", TT, 4 * SLOTS)
        result = area("result", TT, DM)
        w1 = ring[:, 0:RING_W2].rearrange("p (k n) -> p k n", k=KC)
        w2 = ring[:, RING_W2:].rearrange("p (k n) -> p k n", k=KC)

        def chunk_ap(name):
            s = SLOT_OF[name]
            return ring[:, s * KC * NW:(s + 1) * KC * NW].rearrange("p (k n) -> p k n", k=KC)

        x_in, const_in, tables_in, gain_in, gate_in, router_in = ([sem(f"x_in{t}") for t in range(TT)], sem("const_in"),
                                                        sem("tables_in"), sem("gain_in"), sem("gate_in"), sem("router_in"))
        halves_ready, ident_in = sem("halves_ready"), sem("ident_in")
        fq_in = [sem(f"fq_in{j}") for j in range(4)]
        chunk_in = {name: sem(f"{name}_in") for name, _, _ in CHUNKS[1:]}
        wout_in = [sem(f"wout_in{j}") for j in range(2)]
        bias_in, gains_in, aug_in = sem("bias_in"), sem("gains_in"), sem("aug_in")
        psum_full = sem("psum_full")
        freed = {"act": sem("freed_by_act"), "dve": sem("freed_by_dve")}
        dve_done, act_done = sem("dve_done"), sem("act_done")
        xroot_ready, diag_ready, aug_zero, gate_f, neg_f = sem("xroot_ready"), sem("diag_ready"), sem("aug_zero"), sem("gate_f"), sem("neg_f")
        z_abs, z_ln = sem("z_abs"), sem("z_ln")
        max_ready, p_norm = sem("max_ready"), sem("p_norm")
        fkz = sem("fkz")
        ron_ready, h_done, sq_done = sem("ron_ready"), sem("h_done"), sem("sq_done")
        rest_ready, parts_ready, split_done = sem("rest_ready"), sem("parts_ready"), sem("split_done")
        u_ready, rows_ready, pool_done = sem("u_ready"), sem("rows_ready"), sem("pool_done")
        topv_ready, gexp_ready, picked_ready, routed = (
            sem("topv_ready"), sem("gexp_ready"), sem("picked_ready"), sem("routed"))
        w1_in = [sem(f"w1_in{k}") for k in range(KC)]
        w2_in = [sem(f"w2_in{k}") for k in range(KC)]
        w1_used, w2_used = sem("w1_used"), sem("w2_used")
        sel_ready, gath_done, xT_ready = sem("sel_ready"), sem("gath_done"), sem("xT_ready")
        row_ready, rows_used = sem("row_ready"), sem("rows_used")
        h_ready, gm_ready, lc_ready, lg_ready, sg_ready, a_ready = (
            [sem(f"h_ready{n}") for n in range(2)], sem("gm_ready"), sem("lc_ready"), sem("lg_ready"), sem("sg_ready"), sem("a_ready"))
        aT_done, actT_ready, gs_ready, cT_done, cab_ready = (
            sem("aT_done"), sem("actT_ready"), sem("gs_ready"), sem("cT_done"), sem("cab_ready"))
        y_done, y_ready, comb_done, comb_added = sem("y_done"), sem("y_ready"), sem("comb_done"), sem("comb_added")
        zpart_zero, zpart_ready = sem("zpart_zero"), sem("zpart_ready")
        w_rt_ready, root_one = sem("w_rt_ready"), sem("root_one")
        root_ready, seed_ready = sem("root_ready"), sem("seed_ready")
        row_moved = sem("row_moved")
        moved, stored, round_stored = sem("moved"), sem("stored"), sem("round_stored")
        final_sq, final_w, final_seed, final_step, final_ready = (
            sem("final_sq"), sem("final_w"), sem("final_seed"), sem("final_step"), sem("final_ready"))

        x_dram = x[0].rearrange("(t p) d -> p t d", p=P)
        out_dram = out[0].rearrange("(t p) d -> p t d", p=P)
        w_in_dram = w_in[0].rearrange("(k p) n -> p k n", p=P)
        w_out_dram = w_out[0].rearrange("(k p) n -> p k n", p=P)

        def bank(name):
            return psum[:, BANK_OF[name], :]

        def drained(name):
            n = GROUP_AT[name]
            return sum(1 for _, e in GROUPS[:n + 1] if e == GROUPS[n][1])

        def full(name):
            return GROUP_AT[name] + 1

        def free_bank(eng, name):
            for before_name, reader in reversed(GROUPS[:GROUP_AT[name]]):
                if BANK_OF[before_name] == BANK_OF[name]:
                    eng.wait_ge(freed[reader], drained(before_name))
                    break

        Y = BANK_OF["pos"]
        H0, CB = [b for b in range(0, BANKS, 2) if Y not in (b, b + 1)][:2]
        H1 = H0 + 1
        XT, CT, AT = [b for b in range(BANKS) if b not in (Y, H0, H1, CB, CB + 1)]

        block = ctx.enter_context(nc.Block())

        def rounds(eng, body):
            body(0)
            eng.wait_ge(routed, 1)
            need = eng.alloc_register(f"need_{eng.engine.name}")
            eng.reg_load(need, most[0:1, 0:1])
            with eng.If(eng.snap(need) > SLOTS):
                with eng.Fori(1, ROUNDS) as r:
                    with eng.If(eng.snap(need) > r * SLOTS):
                        body(r)

        @block.sync
        def _(sp):
            def load_chunk(name):
                col = {n: cc for n, cc, _ in CHUNKS}[name]
                sp.dma_start(chunk_ap(name), w_in_dram[:, :, col:col + NW]).then_inc(chunk_in[name], 16)

            sp.dma_start(acc[:, 0, :], x_dram[:, 0, :]).then_inc(x_in[0], 16)
            sp.dma_start(g_rows[KC:2 * KC, :], norm_ffn_g[0].rearrange("(k p) -> k p", p=P)).then_inc(gain_in, 16)
            sp.dma_start(acc[:, 1, :], x_dram[:, 1, :]).then_inc(x_in[1], 16)
            for j in range(4):
                k = slice(2 * j, 2 * j + 2)
                sp.dma_start(chunk_ap("fq")[:, k, :], w_in_dram[:, k, CHUNKS[0][1]:CHUNKS[0][1] + NW]).then_inc(fq_in[j], 16)
            sp.dma_start(const[:, P:4 * P], table[:, P:4 * P]).then_inc(const_in, 16)
            sp.dma_start(w_z[:, :, :], w_in_dram[:, :, FZ_COL:FZ_COL + FOX_HEADS]).then_inc(gate_in, 16)
            with nc.allow_non_contiguous_dma(reason="eight words"):
                sp.dma_start(b_fox[:, :], b_forget[0].rearrange("(p a) -> p a", a=1)).then_inc(gate_in, 16)
            for name in ("fk", "rq"):
                load_chunk(name)
            sp.dma_start(const[:, 4 * P:], table[:, 4 * P:]).then_inc(tables_in, 16)
            load_chunk("rk")
            sp.dma_start(w_rt[:, :, :], w_router[0].rearrange("(k p) e -> p k e", p=P)).then_inc(router_in, 16)
            sp.dma_start(b_rt[:, :], b_router[0:1, :].to_broadcast([P, EXPERTS])).then_inc(router_in, 16)
            for j in range(2):
                k0 = OUT_ORDER[4 * j]
                sp.dma_start(w2[:, 4 * j:4 * j + 4, :], w_out_dram[:, k0:k0 + 4, :]).then_inc(wout_in[j], 16)
            for name, gone in (("fv", "fq1"), ("rv", "fk1"), ("rg", "rq1")):
                sp.wait_ge(psum_full, full(gone))
                load_chunk(name)

            def one_round(r):
                with sp.Fori(0, EXPERTS) as e:
                    i = r * EXPERTS + e
                    for k in range(KC):
                        if k < KC - 1:
                            sp.wait_ge(w1_used, (KC - 1) * i + k + 1)
                        else:
                            sp.wait_ge(psum_full, full("rg1"))
                            sp.wait_ge(h_ready[1], i + 1)
                        sp.dma_start(w1[:, k, :], w_exp_in[0, e, k * P:(k + 1) * P, :]).then_inc(w1_in[k], 16)
                    for k in range(KC):
                        if k < KC - 1:
                            sp.wait_ge(w2_used, (KC - 1) * i + k + 1)
                        else:
                            sp.wait_ge(psum_full, full("out3"))
                            sp.wait_ge(y_done, i + 1)
                        sp.dma_start(w2[:, k, :], w_exp_out[0, e, k * P:(k + 1) * P, :]).then_inc(w2_in[k], 16)
                for j, (t, cols) in enumerate(RESULT_PARTS):
                    sp.wait_ge(final_ready, len(RESULT_PARTS) * r + j + 1)
                    sp.dma_start(out_dram[:, t, cols], result[:, t, cols]).then_inc(stored, 16)
                parts = 16 * len(RESULT_PARTS)
                sp.wait_ge(stored, parts * r + parts)
                sp.sem_inc(round_stored, 1)

            rounds(sp, one_round)

        @block.gpsimd
        def _(pool):
            nc.gpsimd.memset(zpart, 0.0).then_inc(zpart_zero, 1)
            pool.wait_ge(zpart_zero, 1)
            nc.gpsimd.memset(augq[0:6, :, :], 1.0).then_inc(aug_zero, 1)
            nc.gpsimd.memset(augk[0:6, :, :], 1.0).then_inc(aug_zero, 1)
            pool.wait_ge(ident_in, 16)
            pool.wait_ge(const_in, 16)
            for half, whole in ((ident_h, ident), (causal_h, causal), (before_h, before), (ones_h, ones)):
                nc.gpsimd.tensor_copy(half[:, :], whole).then_inc(halves_ready, 1)
            pool.wait_ge(aug_zero, 2)
            pool.wait_ge(gate_f, 1)
            for s in range(3):
                pool.dma_start(augq[3 + s:4 + s, :, :], z_parts[:, s, :]).then_inc(aug_in, 16)
            pool.wait_ge(neg_f, 1)
            for s in range(3):
                pool.dma_start(augk[s:s + 1, :, :], z_parts[:, 3 + s, :]).then_inc(aug_in, 16)
            pool.wait_ge(psum_full, full("qk5"))
            for s in range(3):
                rows = bias[s * EXPERTS:(s + 1) * EXPERTS, :]
                pool.dma_start(rows[:, 0:2 * DM], b_exp_in[0]).then_inc(bias_in, 16)
                pool.dma_start(rows[:, 2 * DM:3 * DM], b_exp_out[0]).then_inc(bias_in, 16)
            n = 3 * EXPERTS
            pool.wait_ge(bias_in, 16 * 6)
            pool.wait_ge(psum_full, full("rs3"))
            nc.gpsimd.tensor_copy(bias_part[0:n, :], bias[0:n, :]).then_inc(pool_done, 1)
            pool.wait_ge(pool_done, 1)
            nc.gpsimd.tensor_tensor(bias_rest[0:n, :], bias[0:n, :], bias_part[0:n, :], ALU.subtract).then_inc(pool_done, 1)
            pool.wait_ge(psum_full, full("rg1"))
            pool.dma_start(area("g_ffn"), norm_ffn_g[0:1, :].to_broadcast([P, DM])).then_inc(gains_in, 16)
            pool.dma_start(area("g_final"), norm_final_g.rearrange("(a d) -> a d", a=1).to_broadcast([P, DM])) \
                .then_inc(gains_in, 16)
            pool.wait_ge(psum_full, full("pv1"))
            pool.wait_ge(pool_done, 2)
            nc.gpsimd.memset(y, 0.0).then_inc(pool_done, 1)
            pool.wait_ge(pool_done, 3)
            pool.dma_start(bias_rows[0:EXPERTS, :], bias_part[0:EXPERTS, :]).then_inc(row_moved, 16)
            pool.wait_ge(row_moved, 16)
            nc.gpsimd.tensor_copy(bias_part[0:n, :], bias_rest[0:n, :]).then_inc(pool_done, 1)
            pool.wait_ge(pool_done, 4)
            pool.dma_start(bias_rows[EXPERTS:2 * EXPERTS, :], bias_part[EXPERTS:2 * EXPERTS, :]).then_inc(row_moved, 16)
            nc.gpsimd.tensor_tensor(bias_rows[2 * EXPERTS:n, :], bias_rest[2 * EXPERTS:n, :],
                                    bias_part[2 * EXPERTS:n, :], ALU.subtract).then_inc(rows_ready, 1)
            pool.wait_ge(rows_ready, 1)
            pool.wait_ge(parts_ready, 1)
            nc.gpsimd.tensor_tensor(u_parts[:, 2, 0, :], u_rest[:, 0, :], u_parts[:, 1, 0, :], ALU.subtract) \
                .then_inc(split_done, 1)

        @block.tensor
        def _(pe):
            mm = nc.tensor.matmul
            for first in (cT_done, rows_used, y_done, h_ready[1]):
                pe.sem_inc(first, 1)

            def transposes(name, pieces):
                for j, piece in enumerate(pieces):
                    ins = nc.tensor.transpose(bank(name)[:, j * P:(j + 1) * P], piece, ident)
                ins.then_inc(psum_full, 1)

            def project(name):
                if name != "fq":
                    pe.wait_ge(chunk_in[name], 16)
                for t in range(TT):
                    free_bank(pe, f"{name}{t}")
                    if name == "fq":
                        pe.wait_ge(freed["act"], drained(f"uT{t}0"))
                        pe.wait_ge(freed["dve"], drained(f"uT{t}1"))
                    for k in range(KC):
                        if name == "fq" and t == 0 and k % 2 == 0:
                            pe.wait_ge(fq_in[k // 2], 16)
                        ins = mm(bank(f"{name}{t}"), uT[:, k, t * P:(t + 1) * P], chunk_ap(name)[:, k, :],
                                 start=(k == 0), stop=(k == KC - 1))
                    ins.then_inc(psum_full, 1)

            pe.wait_ge(ident_in, 16)
            pe.wait_ge(gain_in, 32)
            nc.tensor.transpose(bank("gT")[:, 0:2 * KC], g_rows[:, :], ident[0:2 * KC, 0:2 * KC]).then_inc(psum_full, 1)
            for t in range(TT):
                pe.wait_ge(x_in[t], 16)
                for g in range(2):
                    transposes(f"uT{t}{g}", [acc[:, t, k * P:(k + 1) * P] for k in range(4 * g, 4 * g + 4)])
            project("fq")

            pe.wait_ge(const_in, 16)
            pe.wait_ge(diag_ready, TT)
            for t in range(TT):
                ins = mm(bank("rr")[0:FOX_HEADS, t * P:(t + 1) * P], ones[:, 0:FOX_HEADS], diag[:, t, :],
                         start=True, stop=True)
            ins.then_inc(psum_full, 1)
            pe.wait_ge(gate_in, 32)
            free_bank(pe, "zp")
            for k in range(KC):
                at = (k % 4) * 32
                ins = mm(bank("zp")[at:at + FOX_HEADS, 0:SEQ], w_z[:, k, :], uT[:, k, :],
                         start=(k < 4), stop=(k >= 4), tile_position=(0, at))
            ins.then_inc(psum_full, 1)

            project("fk")
            pe.wait_ge(tables_in, 16)
            pe.wait_ge(zpart_ready, 4)
            free_bank(pe, "fz")
            mm(bank("fz")[0:FOX_HEADS, 0:SEQ], stack[:, 0:FOX_HEADS], zpart, start=True, stop=True).then_inc(psum_full, 1)
            pe.wait_ge(freed["act"], drained("fq1"))
            for t in range(TT):
                free_bank(pe, f"fqT{t}")
                transposes(f"fqT{t}", [fq[:, t, j * P:(j + 1) * P] for j in range(4)])
            project("rq")
            pe.wait_ge(freed["act"], drained("fk1"))
            for t in range(TT):
                free_bank(pe, f"fkT{t}")
                transposes(f"fkT{t}", [fk[:, t, j * P:(j + 1) * P] for j in range(4)])
            project("rk")

            pe.wait_ge(freed["dve"], drained("fqT1"))
            pe.wait_ge(freed["act"], drained("fkT1"))
            pe.wait_ge(fkz, 2)
            pe.wait_ge(aug_in, 16 * 6)
            pe.wait_ge(halves_ready, 2)
            for g, (t, h0, nh, keys) in enumerate(QK_GROUPS):
                free_bank(pe, f"qk{g}")
                tile = bank(f"qk{g}").rearrange("p (h s) -> p h s", h=nh)
                for j in range(nh):
                    h = h0 + j
                    kT = fkTo if h % 2 else fkTe
                    q = slice(t * P, (t + 1) * P)
                    mm(tile[:, j, :], fqT[:, h // 2, q], kT[:, h // 2, 0:keys], start=True, stop=False)
                    mm(tile[:, j, q], ident_h[:, :], causal_h[:, :], start=False, stop=False, skip_group_check=True)
                    ins = mm(tile[:, j, :], augq[0:6, h, q], augk[0:6, h, 0:keys], start=False, stop=True)
                ins.then_inc(psum_full, 1)

            project("fv")
            for name, src in (("rqT", rq), ("rkT", rk)):
                pe.wait_ge(dve_done, DVE_ROTATED)
                for t in range(TT):
                    free_bank(pe, f"{name}{t}")
                    transposes(f"{name}{t}", [src[:, t, h * P:(h + 1) * P] for h in range(RET_HEADS)])
            project("rv")
            pe.wait_ge(psum_full, full("fv1"))
            pe.sem_inc(w1_used, 2)
            for g, (t, s, h0) in enumerate(PT_GROUPS):
                pe.wait_ge(p_norm, 2 if t == 0 else 6)
                free_bank(pe, f"pT{g}")
                base, width = (0, P) if t == 0 else (TT * NW, SEQ)
                transposes(f"pT{g}", [p_w[:, base + h * width + s * P:base + h * width + s * P + P]
                                      for h in range(h0, h0 + 4)])

            pe.wait_ge(freed["dve"], drained("rqT1"))
            pe.wait_ge(freed["act"], drained("rkT1"))
            for h in range(RET_HEADS):
                free_bank(pe, f"rs{h}")
                mm(bank(f"rs{h}")[:, 0:SEQ], rkT[:, h, 0:P], rqT[:, h, :], start=True, stop=True)
                mm(bank(f"rs{h}")[:, SEQ:384], rkT[:, h, P:SEQ], rqT[:, h, P:SEQ], start=True, stop=True) \
                    .then_inc(psum_full, 1)
            pe.wait_ge(psum_full, full("rv1"))
            pe.sem_inc(w1_used, 2)
            project("rg")

            pe.wait_ge(freed["act"], drained("pT4"))
            pe.wait_ge(freed["dve"], drained("pT5"))
            for g in range(2):
                free_bank(pe, f"pv{g}")
                tile = bank(f"pv{g}").rearrange("p (j t) -> p j t", j=2)
                for jj in range(2):
                    for half in range(2):
                        h = 2 * (2 * g + jj) + half
                        rows = slice(half * FOX_D, (half + 1) * FOX_D)
                        v = slice(h * FOX_D, (h + 1) * FOX_D)
                        mm(tile[rows, jj, :], fv[:, 0, v], pT0[:, h, :], start=True, stop=True)
                        ins = mm(tile[rows, jj, P:SEQ], fv[:, 1, v], pT1[:, h, :], start=False, stop=True,
                                 skip_group_check=True)
                ins.then_inc(psum_full, 1)

            pe.wait_ge(psum_full, full("rg1"))
            pe.sem_inc(w1_used, 3)

            pe.wait_ge(freed["dve"], drained("rs3"))
            pe.wait_ge(freed["act"], drained("rv1"))
            for t in range(TT):
                free_bank(pe, f"ro{t}")
                for h in range(RET_HEADS):
                    d = slice(h * P, (h + 1) * P)
                    o = bank(f"ro{t}")[:, d]
                    if t == 0:
                        ins = mm(o, rsc[:, h, 0:P], rv[:, 0, d], start=True, stop=True)
                    else:
                        mm(o, rsc[:, h, P:SEQ], rv[:, 0, d], start=True, stop=False)
                        ins = mm(o, rsc[:, h, SEQ:384], rv[:, 1, d], start=False, stop=True)
                ins.then_inc(psum_full, 1)

            def out_chunk(j, t):
                for n in range(2):
                    ins = mm(bank(f"out{2 * t + n}"), mixT[:, OUT_ORDER[j], t * P:(t + 1) * P],
                             w2[:, j, n * NW:(n + 1) * NW], start=(j == 0), stop=(j == KC - 1))
                    if j == KC - 1:
                        ins.then_inc(psum_full, 1)
                return ins

            for g in range(4):
                free_bank(pe, f"out{g}")
            pe.wait_ge(freed["act"], drained("pv1"))
            pe.wait_ge(wout_in[0], 16)

            def turn_retention(t):
                pe.wait_ge(ron_ready, t + 1)
                free_bank(pe, f"rT{t}")
                transposes(f"rT{t}", [on[:, t, h * P:(h + 1) * P] for h in range(RET_HEADS)])

            for j in range(4):
                if j == 3:
                    turn_retention(0)
                out_chunk(j, 0)
                out_chunk(j, 1).then_inc(w2_used, 1)
            turn_retention(1)
            pe.wait_ge(freed["act"], drained("rT0"))
            pe.wait_ge(wout_in[1], 16)
            for j in range(4, KC):
                out_chunk(j, 0)

            def turn_h(t):
                pe.wait_ge(h_done, t + 1)
                for g in range(2):
                    free_bank(pe, f"hT{t}{g}")
                    transposes(f"hT{t}{g}", [acc[:, t, k * P:(k + 1) * P] for k in range(4 * g, 4 * g + 4)])

            def part_logits(t):
                free_bank(pe, f"part{t}")
                for k in range(KC):
                    if k % 4 == 0:
                        name = f"hT{t}{k // 4}"
                        pe.wait_ge(freed[GROUPS[GROUP_AT[name]][1]], drained(name))
                    at = (k % 4) * EXPERTS
                    ins = mm(bank(f"part{t}")[at:at + EXPERTS, 0:P], w_rt[:, k, :], hT[:, k, t * P:(t + 1) * P],
                             start=(k < 4), stop=(k >= 4), tile_position=(0, at))
                ins.then_inc(psum_full, 1)

            def sum_logits(t):
                pe.wait_ge(freed["act"], drained(f"part{t}"))
                free_bank(pe, f"logits{t}")
                mm(bank(f"logits{t}")[:, 0:EXPERTS], partial[:, t, :], stack, start=True, stop=True).then_inc(psum_full, 1)

            pe.wait_ge(w_rt_ready, 1)
            pe.wait_ge(tables_in, 16)
            pe.wait_ge(freed["act"], drained("rT1"))
            for j in range(4, KC):
                ins = out_chunk(j, 1)
                if j < KC - 1:
                    ins.then_inc(w2_used, 1)
                if j == KC - 3:
                    turn_h(0)
                if j == KC - 2:
                    part_logits(0)
            sum_logits(0)
            turn_h(1)
            part_logits(1)
            sum_logits(1)

            def stay_awake():
                for _ in range(WAKING):
                    mm(bank("part1")[:, 0:P], ident_h[:, :], before_h[:, :], start=True, stop=True)
            pe.wait_ge(halves_ready, 4)
            stay_awake()
            pe.wait_ge(picked_ready, 2)
            free_bank(pe, "pos")
            pos = bank("pos")
            mm(pos[:, 0:32], before_h[:, :], picked[:, 0, :], start=True, stop=True)
            mm(pos[:, 32:64], ones_h[:, :], picked[:, 0, :], start=True, stop=False)
            mm(pos[:, 32:64], before_h[:, :], picked[:, 1, :], start=False, stop=True)
            mm(pos[:, 64:96], ones_h[:, :], picked[:, 0, :], start=True, stop=False)
            mm(pos[:, 64:96], ones_h[:, :], picked[:, 1, :], start=False, stop=True).then_inc(psum_full, 1)

            def gather():
                for k in range(KC):
                    n = 0
                    for s in range(3):
                        for t in range(TT):
                            ins = mm(psum[:, XT, k * SLOTS:(k + 1) * SLOTS], u_parts[:, s, t, k * P:(k + 1) * P],
                                     sel[:, t, :], start=(n == 0), stop=(n == 5))
                            n += 1
                ins.then_inc(gath_done, 1)

            def combine(t, at):
                for half in range(2):
                    ins = mm(psum[:, at + half, :], cab[:, 2 * half + t, :], y, start=True, stop=True)
                ins.then_inc(comb_done, 1)

            def one_round(r):
                g0 = r * (EXPERTS + 1)
                pe.wait_ge(comb_added, 2 * g0 + 1)
                pe.wait_ge(sel_ready, g0 + 1)
                gather()
                pe.wait_ge(routed, 1)
                pe.wait_ge(rows_ready, 1)
                pe.wait_ge(row_moved, 32)
                with pe.Fori(0, EXPERTS) as e:
                    i = r * EXPERTS + e
                    g = r * (EXPERTS + 1) + e
                    pe.wait_ge(xT_ready, g + 1)
                    pe.wait_ge(lc_ready, i + 1)
                    for k in range(KC):
                        pe.wait_ge(w1_in[k], 16 * i + 16)
                        for n in range(2):
                            for half in range(2):
                                cols = slice((2 * n + half) * NW, (2 * n + half + 1) * NW)
                                ins = mm(psum[half * 64:half * 64 + 64, H0 + n, :], xT[:, k, :], w1[:, k, cols],
                                         start=(k == 0), stop=(k == KC - 1))
                            if k == KC - 1:
                                ins.then_inc(h_ready[n], 1)
                        if k < KC - 1:
                            ins.then_inc(w1_used, 1)
                        if k == 2:
                            pe.wait_ge(y_ready, i + 1)
                            pe.wait_ge(cab_ready, i + r + 1)
                            pe.wait_ge(comb_added, 2 * g + 1)
                            combine(0, CB)
                        if k == 3:
                            pe.wait_ge(row_ready, i + 1)
                            for n in range(2):
                                for half in range(2):
                                    cols = slice((2 * n + half) * NW, (2 * n + half + 1) * NW)
                                    mm(psum[half * 64:half * 64 + 64, H0 + n, :], sel_row[:, :],
                                       bias_rows[0:3 * EXPERTS, cols], start=False, stop=False)
                        if k == 5:
                            pe.wait_ge(sel_ready, g + 2)
                            gather()
                    for half in range(2):
                        ins = mm(psum[half * 64:half * 64 + 64, Y, :], sel_row[:, :],
                                 bias_rows[0:3 * EXPERTS, 2 * DM + half * NW:2 * DM + (half + 1) * NW],
                                 start=True, stop=False)
                    ins.then_inc(rows_used, 1)
                    pe.wait_ge(comb_added, 2 * g + 2)
                    combine(1, CB)
                    pe.wait_ge(a_ready, i + 1)
                    for j in range(4):
                        ins = nc.tensor.transpose(psum[:, AT, j * P:(j + 1) * P], act[:, j * P:(j + 1) * P], ident)
                    ins.then_inc(aT_done, 1)
                    pe.wait_ge(gs_ready, i + 1)
                    for j in range(4):
                        ins = nc.tensor.transpose(psum[:, CT, j * P:(j + 1) * P],
                                                  gs[:, j % 2, (j // 2) * P:(j // 2 + 1) * P], ident)
                    ins.then_inc(cT_done, 1)
                    pe.wait_ge(actT_ready, i + 1)
                    for k in range(KC):
                        pe.wait_ge(w2_in[k], 16 * i + 16)
                        for half in range(2):
                            lhs = actT[:, k % 4, (k // 4) * SLOTS:(k // 4 + 1) * SLOTS]
                            ins = mm(psum[half * 64:half * 64 + 64, Y, :], lhs, w2[:, k, half * NW:(half + 1) * NW],
                                     start=False, stop=(k == KC - 1))
                        if k < KC - 1:
                            ins.then_inc(w2_used, 1)
                    ins.then_inc(y_done, 1)
                pe.wait_ge(y_ready, (r + 1) * EXPERTS + 1)
                pe.wait_ge(cab_ready, (r + 1) * EXPERTS + r + 1)
                pe.wait_ge(comb_added, 2 * (g0 + EXPERTS) + 1)
                combine(0, CB)
                pe.wait_ge(lc_ready, (r + 1) * EXPERTS + 1)
                combine(1, H0)

            stay_awake()
            pe.wait_ge(parts_ready, 3)
            pe.wait_ge(split_done, TT)
            rounds(pe, one_round)

        @block.scalar
        def _(eng):
            eng.sem_inc(y_ready, 1)
            eng.dma_start(const[:, 0:P], table[:, 0:P]).then_inc(ident_in, 16)
            eng.dma_start(g_rows[0:KC, :], norm_mix_g[0].rearrange("(k p) -> k p", p=P)).then_inc(gain_in, 16)

            act_i = nc.scalar.activation

            def copy(o, i, scale=1.0):
                return act_i(o, i, ACT.Copy, scale=scale)

            eng.wait_ge(root_one, 1)
            act_i(root_sqrt[:, 0:1], root_of[:, 0:1], ACT.Sqrt)
            def square_roots(event):
                cols = ROOT_COLS[event]
                eng.wait_ge(root_ready, event + 1)
                act_i(root_sqrt[:, cols], root_of[:, cols], ACT.Sqrt).then_inc(seed_ready, 1)

            def scaled_uT(t):
                eng.wait_ge(psum_full, full(f"uT{t}0"))
                for k in range(4):
                    ins = copy(uT[:, k, t * P:(t + 1) * P], bank(f"uT{t}0")[:, k * P:(k + 1) * P], scale=g_cols[:, k:k + 1])
                ins.then_inc(freed["act"], 1)

            def read(name, o, i, scale=1.0):
                eng.wait_ge(psum_full, full(name))
                copy(o, i, scale).then_inc(freed["act"], 1)

            def four(name):
                return bank(name).rearrange("p (j t) -> p j t", j=4)

            eng.wait_ge(freed["dve"], drained("gT"))
            scaled_uT(0)
            scaled_uT(1)
            eng.wait_ge(x_in[0], 16)
            act_i(scratch[:, 0, :], acc[:, 0, :], ACT.Square, accum_out=ss[:, 0:1]).then_inc(sq_done, 1)
            square_roots(0)
            eng.wait_ge(xroot_ready, 2)
            for t in range(TT):
                read(f"fq{t}", fq[:, t, :], bank(f"fq{t}"), scale=root_eighth[:, t:t + 1])
            for t in range(TT):
                read(f"fk{t}", fk[:, t, :], bank(f"fk{t}"), scale=inv_root[:, t:t + 1])
            z_neg, z_exp, z_log = zwork[0:FOX_HEADS, 1, :], zwork[0:FOX_HEADS, 2, :], zwork[0:FOX_HEADS, 3, :]
            eng.wait_ge(z_abs, 1)
            act_i(z_exp, z_neg, ACT.Exp).then_inc(act_done, 1)
            eng.wait_ge(act_done, 1)
            act_i(z_log, z_exp, ACT.Ln, bias=1.0).then_inc(z_ln, 1)
            for t in range(TT):
                eng.wait_ge(psum_full, full(f"fkT{t}"))
                cols = slice(t * P, (t + 1) * P)
                copy(fkTe[0:FOX_D, :, cols], four(f"fkT{t}")[0:FOX_D, :, :])
                copy(fkTo[FOX_D:P, :, cols], four(f"fkT{t}")[FOX_D:P, :, :]).then_inc(freed["act"], 1)
            for g, (t, h0, nh, keys) in enumerate(QK_GROUPS):
                eng.wait_ge(max_ready, g + 1)
                base = 0 if t == 0 else TT * NW
                for j in range(nh):
                    h, col = h0 + j, t * FOX_HEADS + h0 + j
                    ins = act_i(p_w[:, base + h * keys:base + (h + 1) * keys], bank(f"qk{g}")[:, j * keys:(j + 1) * keys],
                                ACT.Exp, bias=negmax[:, col:col + 1], accum_out=psum_p[:, col:col + 1])
                ins.then_inc(freed["act"], 1)
            for t in range(TT):
                read(f"fv{t}", fv[:, t, :], bank(f"fv{t}"), scale=inv_root[:, t:t + 1])
            for t in range(TT):
                read(f"rkT{t}", rkT[:, :, t * P:(t + 1) * P], four(f"rkT{t}"))
            for t in range(TT):
                read(f"rv{t}", rv[:, t, :], bank(f"rv{t}"), scale=inv_root[:, t:t + 1])

            def read_pT(g):
                t, s, h0 = PT_GROUPS[g]
                dst = pT1[:, h0:h0 + 4, :] if s else pT0[:, h0:h0 + 4, t * P:(t + 1) * P]
                read(f"pT{g}", dst, four(f"pT{g}"))

            for g in (0, 2, 4):
                read_pT(g)
            for t in range(TT):
                eng.wait_ge(psum_full, full(f"rg{t}"))
                act_i(eg[:, t, :], bank(f"rg{t}"), ACT.Exp, scale=minus_root[:, t:t + 1])
                copy(rg[:, t, :], bank(f"rg{t}"), scale=inv_root[:, t:t + 1]).then_inc(freed["act"], 1)
            for g in range(2):
                read(f"pv{g}", mixT[:, 4 + 2 * g:6 + 2 * g, :], bank(f"pv{g}").rearrange("p (j t) -> p j t", j=2))
            for t in range(TT):
                square_roots(1 + t)
            for t in range(TT):
                read(f"rT{t}", mixT[:, 0:RET_HEADS, t * P:(t + 1) * P], four(f"rT{t}"))
            def square_h(t):
                eng.wait_ge(h_done, t + 1)
                act_i(u[:, t, :], acc[:, t, :], ACT.Square, accum_out=ss[:, TT + t:TT + t + 1]).then_inc(sq_done, 1)

            def read_hT(name):
                t, g = int(name[2]), int(name[3])
                read(name, hT[:, 4 * g:4 * g + 4, t * P:(t + 1) * P], four(name))

            def read_part(t):
                read(f"part{t}", partial[:, t, :], bank(f"part{t}")[:, 0:P])

            square_h(0)
            square_roots(3)
            read_hT("hT00")
            read_hT("hT01")
            eng.wait_ge(rest_ready, 1)
            copy(u_parts[:, 1, 0, :], u_rest[:, 0, :]).then_inc(parts_ready, 1)
            read_part(0)
            square_h(1)
            read_hT("hT10")
            square_roots(4)
            read_hT("hT11")
            read_part(1)
            eng.wait_ge(u_ready, TT)
            copy(u_parts[:, 0, 1, :], u[:, 1, :]).then_inc(parts_ready, 1)
            eng.wait_ge(rest_ready, 2)
            copy(u_parts[:, 1, 1, :], u_rest[:, 1, :]).then_inc(parts_ready, 1)
            for t in range(TT):
                eng.wait_ge(topv_ready, t + 1)
                act_i(gate4[:, t, :], top_v[:, t, 0:TOP_K], ACT.Exp, bias=negtop[:, t:t + 1],
                      accum_out=gsum[:, t:t + 1]).then_inc(gexp_ready, 1)

            def read_xT():
                copy(xT[:, :, :], psum[:, XT, :].rearrange("p (k s) -> p k s", k=KC)).then_inc(xT_ready, 1)

            def one_round(r):
                g0 = r * (EXPERTS + 1)
                eng.wait_ge(gath_done, g0 + 1)
                read_xT()
                with eng.Fori(0, EXPERTS) as e:
                    i = r * EXPERTS + e
                    g = r * (EXPERTS + 1) + e
                    eng.wait_ge(gm_ready, i + 1)
                    act_i(sg, gm, ACT.Sigmoid, scale=ALPHA).then_inc(sg_ready, 1)
                    eng.wait_ge(h_ready[1], i + 2)
                    eng.wait_ge(gath_done, g + 2)
                    read_xT()
                    eng.wait_ge(aT_done, i + 1)
                    copy(actT[:, :, :], psum[:, AT, :].rearrange("p (j q) -> p j q", j=4)).then_inc(actT_ready, 1)
                    eng.wait_ge(cT_done, i + 2)
                    eng.wait_ge(comb_done, 2 * g + 2)
                    copy(cab[:, :, :], psum[:, CT, :].rearrange("p (j q) -> p j q", j=4)).then_inc(cab_ready, 1)
                    eng.wait_ge(y_done, i + 2)
                    copy(y, psum[:, Y, :]).then_inc(y_ready, 1)
                eng.wait_ge(comb_added, 2 * (g0 + EXPERTS) + 2)
                act_i(result[:, 0, :], acc[:, 0, :], ACT.Square, accum_out=ss[:, 0:1]).then_inc(final_sq, 1)
                eng.wait_ge(final_w, r + 1)
                act_i(root_sqrt[:, ROOT_COLS[5]], root_of[:, ROOT_COLS[5]], ACT.Sqrt).then_inc(final_seed, 1)

            rounds(eng, one_round)

        @block.vector
        def _(dve):
            v = nc.vector
            steps = [0]
            for first in (lc_ready, comb_added):
                dve.sem_inc(first, 1)

            def then(ins):
                steps[0] += 1
                ins.then_inc(dve_done, 1)
                dve.wait_ge(dve_done, steps[0])

            def inverse_roots(event, square, scale, eps):
                cols = ROOT_COLS[event]
                w, r, t = root_of[:, cols], inv_root[:, cols], root_t[:, cols]
                if event:
                    dve.wait_ge(root_ready, event)
                v.tensor_scalar(w, square, scale, eps, ALU.mult, ALU.add).then_inc(root_ready, 1)
                dve.wait_ge(seed_ready, event + 1)
                then(v.reciprocal(r, root_sqrt[:, cols]))
                then(v.tensor_tensor(t, r, r, ALU.mult))
                then(v.tensor_tensor(t, t, w, ALU.mult))
                then(v.tensor_scalar(t, t, -0.5, 1.5, ALU.mult, ALU.add))
                then(v.tensor_tensor(r, r, t, ALU.mult))

            v.memset(root_of[:, 0:1], 1.0).then_inc(root_one, 1)
            v.memset(fkTe[FOX_D:P, :, :], 0.0).then_inc(fkz, 1)
            v.memset(fkTo[0:FOX_D, :, :], 0.0).then_inc(fkz, 1)
            then(v.memset(slot_of[:, :, :], -UNPICKED))
            dve.wait_ge(psum_full, full("gT"))
            v.tensor_copy(g_cols[:, :], bank("gT")[:, 0:2 * KC]).then_inc(freed["dve"], 1)
            dve.wait_ge(freed["dve"], drained("gT"))
            for t in range(TT):
                dve.wait_ge(psum_full, full(f"uT{t}1"))
                for k in range(4, KC):
                    ins = v.tensor_scalar(uT[:, k, t * P:(t + 1) * P], bank(f"uT{t}1")[:, (k - 4) * P:(k - 3) * P],
                                          g_cols[:, k:k + 1], None, ALU.mult)
                ins.then_inc(freed["dve"], 1)
            dve.wait_ge(x_in[1], 16)
            then(v.tensor_tensor_reduce(scratch[:, 1, :], acc[:, 1, :], acc[:, 1, :], 1.0, 0.0, ALU.mult, ALU.add, ss[:, 1:2]))
            dve.wait_ge(sq_done, 1)
            inverse_roots(0, ss[:, 0:TT], 1.0 / DM, RMS_EPS)
            v.tensor_scalar(root_eighth[:, :], inv_root[:, 0:TT], FOX_D ** -0.5, None, ALU.mult).then_inc(xroot_ready, 1)
            v.tensor_scalar(minus_root[:, :], inv_root[:, 0:TT], -1.0, None, ALU.mult).then_inc(xroot_ready, 1)
            dve.wait_ge(ident_in, 16)
            for t in range(TT):
                v.tensor_scalar(diag[:, t, :], ident, inv_root[:, t:t + 1], None, ALU.mult).then_inc(diag_ready, 1)

            zb, zneg, zlog, zls, zf, znf = (zwork[0:FOX_HEADS, j, :] for j in (0, 1, 3, 4, 5, 6))
            dve.wait_ge(gate_in, 32)
            dve.wait_ge(psum_full, full("rr"))
            v.tensor_copy(zneg, bank("rr")[0:FOX_HEADS, 0:SEQ]).then_inc(freed["dve"], 1)
            dve.wait_ge(psum_full, full("zp"))
            dve.wait_ge(zpart_zero, 1)
            for j in range(4):
                rows = slice(32 * j, 32 * j + FOX_HEADS)
                v.tensor_copy(zpart[rows, :], bank("zp")[rows, 0:SEQ]).then_inc(zpart_ready, 1)
            dve.wait_ge(zpart_ready, 4)
            dve.sem_inc(freed["dve"], 1)
            dve.wait_ge(psum_full, full("fz"))
            dve.wait_ge(freed["dve"], drained("rr"))
            v.tensor_tensor(zb, bank("fz")[0:FOX_HEADS, 0:SEQ], zneg, ALU.mult).then_inc(freed["dve"], 1)
            dve.wait_ge(freed["dve"], drained("fz"))
            then(v.tensor_scalar(zb, zb, b_fox[:, 0:1], None, ALU.add))
            v.scalar_tensor_tensor(out=zneg, in0=zb, scalar=-1.0, in1=zb, op0=ALU.mult, op1=ALU.min).then_inc(z_abs, 1)
            dve.wait_ge(z_ln, 1)
            then(v.scalar_tensor_tensor(out=zls, in0=zb, scalar=0.0, in1=zlog, op0=ALU.min, op1=ALU.subtract))
            dve.wait_ge(const_in, 16)
            then(v.tensor_tensor_scan(zf, const[0:FOX_HEADS, CONST_AT["ones"][0]:CONST_AT["ones"][0] + 1].to_broadcast([FOX_HEADS, SEQ]),
                                      zls, 0.0, ALU.mult, ALU.add))
            then(v.tensor_copy(z_parts[:, 0, :], zf))
            then(v.tensor_tensor(znf, zf, z_parts[:, 0, :], ALU.subtract))
            then(v.tensor_copy(z_parts[:, 1, :], znf))
            v.tensor_tensor(z_parts[:, 2, :], znf, z_parts[:, 1, :], ALU.subtract).then_inc(gate_f, 1)
            dve.wait_ge(gate_f, 1)
            v.tensor_scalar(z_parts[:, 3:6, :], z_parts[:, 0:3, :], -1.0, None, ALU.mult).then_inc(neg_f, 1)

            def four(name):
                return bank(name).rearrange("p (j t) -> p j t", j=4)

            def read(name, o, i):
                dve.wait_ge(psum_full, full(name))
                v.tensor_copy(o, i).then_inc(freed["dve"], 1)

            for t in range(TT):
                read(f"fqT{t}", fqT[:, :, t * P:(t + 1) * P], four(f"fqT{t}"))

            def rotate(name, dst, t):
                dve.wait_ge(psum_full, full(name))
                src = bank(name).rearrange("p (h a j) -> p h a j", h=RET_HEADS, a=2)
                part = rot[:, 0, :].rearrange("p (h a j) -> p h a j", h=RET_HEADS, a=2)
                turn = rot[:, 1, :].rearrange("p (h a j) -> p h a j", h=RET_HEADS, a=2)
                shape = [P, RET_HEADS, 64]

                def scaled(o, i, angles):
                    return v.scalar_tensor_tensor(out=o, in0=i, scalar=inv_root[:, t:t + 1],
                                                  in1=angles[:, t:t + 1, :].to_broadcast(shape), op0=ALU.mult, op1=ALU.mult)

                for a in range(2):
                    scaled(part[:, :, a, :], src[:, :, a, :], cos)
                scaled(turn[:, :, 0, :], src[:, :, 1, :], negsin)
                scaled(turn[:, :, 1, :], src[:, :, 0, :], sin).then_inc(freed["dve"], 1)
                dve.wait_ge(freed["dve"], drained(name))
                then(v.tensor_tensor(dst[:, t, :], rot[:, 0, :], rot[:, 1, :], ALU.add))

            dve.wait_ge(tables_in, 16)
            for name, dst in (("rq", rq), ("rk", rk)):
                for t in range(TT):
                    rotate(f"{name}{t}", dst, t)
            assert steps[0] == DVE_ROTATED
            dve.wait_ge(router_in, 32)
            v.tensor_tensor(w_rt[:, :, :], w_rt[:, :, :],
                            g_cols[:, KC:2 * KC].rearrange("p (k a) -> p k a", a=1).to_broadcast([P, KC, EXPERTS]),
                            ALU.mult).then_inc(w_rt_ready, 1)

            for g, (t, h0, nh, keys) in enumerate(QK_GROUPS):
                dve.wait_ge(psum_full, full(f"qk{g}"))
                col = t * FOX_HEADS + h0
                v.tensor_reduce(negmax[:, col:col + nh], bank(f"qk{g}").rearrange("p (h s) -> p h s", h=nh),
                                AX.X, ALU.max, negate=True).then_inc(max_ready, 1)
            for g, (t, h0, nh, keys) in enumerate(QK_GROUPS):
                dve.wait_ge(freed["act"], drained(f"qk{g}"))
                col = t * FOX_HEADS + h0
                base = (0 if t == 0 else TT * NW) + h0 * keys
                tile = p_w[:, base:base + nh * keys].rearrange("p (h s) -> p h s", h=nh)
                then(v.reciprocal(rsum_p[:, col:col + nh], psum_p[:, col:col + nh]))
                scale = rsum_p[:, col:col + nh].rearrange("p (h a) -> p h a", a=1).to_broadcast([P, nh, keys])
                v.tensor_tensor(tile, tile, scale, ALU.mult).then_inc(p_norm, 1)
            for t in range(TT):
                read(f"rqT{t}", rqT[:, :, t * P:(t + 1) * P], four(f"rqT{t}"))
            for g in (1, 3, 5):
                t, s, h0 = PT_GROUPS[g]
                dst = pT1[:, h0:h0 + 4, :] if s else pT0[:, h0:h0 + 4, t * P:(t + 1) * P]
                read(f"pT{g}", dst, four(f"pT{g}"))
            for h in range(RET_HEADS):
                dve.wait_ge(psum_full, full(f"rs{h}"))
                v.tensor_tensor(rsc[:, h, :], bank(f"rs{h}")[:, 0:384], decay[:, h, :], ALU.mult) \
                    .then_inc(freed["dve"], 1)
            dve.wait_ge(freed["act"], drained("rg1"))
            then(v.tensor_scalar(area("eg"), area("eg"), 1.0, None, ALU.add))
            then(v.reciprocal(area("eg"), area("eg")))
            then(v.tensor_tensor(area("rg"), area("rg"), area("eg"), ALU.mult))
            for t in range(TT):
                dve.wait_ge(psum_full, full(f"ro{t}"))
                tile = bank(f"ro{t}").rearrange("p (h d) -> p h d", h=RET_HEADS)
                for h in range(RET_HEADS):
                    ins = v.bn_stats(stats[:, h, :], tile[:, h, :])
                then(ins)
                for h in range(RET_HEADS):
                    ins = v.bn_aggr(mv[:, h, :], stats[:, h, :])
                then(ins)
                inverse_roots(1 + t, mv[:, :, 1], 1.0, GN_EPS)
                for h in range(RET_HEADS):
                    ins = v.tensor_scalar(on[:, t, h * P:(h + 1) * P], tile[:, h, :], mv[:, h, 0:1],
                                          inv_root[:, ROOT_COLS[1 + t].start + h:ROOT_COLS[1 + t].start + h + 1], ALU.subtract, ALU.mult)
                ins.then_inc(freed["dve"], 1)
                dve.wait_ge(freed["dve"], drained(f"ro{t}"))
                v.tensor_tensor(on[:, t, :], on[:, t, :], rg[:, t, :], ALU.mult).then_inc(ron_ready, 1)

            def add_mix(t):
                for n in range(2):
                    g = 2 * t + n
                    dve.wait_ge(psum_full, full(f"out{g}"))
                    cols = slice(n * NW, (n + 1) * NW)
                    v.tensor_tensor(acc[:, t, cols], acc[:, t, cols], bank(f"out{g}"), ALU.add).then_inc(freed["dve"], 1)
                dve.wait_ge(freed["dve"], drained(f"out{2 * t + 1}"))
                dve.sem_inc(h_done, 1)

            def h_roots(t):
                dve.wait_ge(sq_done, 2 + t)
                inverse_roots(3 + t, ss[:, TT + t:TT + t + 1], 1.0 / DM, RMS_EPS)

            def norm_h(t):
                v.scalar_tensor_tensor(out=u[:, t, :], in0=acc[:, t, :], scalar=inv_root[:, ROOT_COLS[3 + t]],
                                       in1=area("g_ffn"), op0=ALU.mult, op1=ALU.mult).then_inc(u_ready, 1)
                dve.wait_ge(u_ready, t + 1)

            def u_less_part0(t):
                v.tensor_tensor(u_rest[:, t, :], u[:, t, :], u_parts[:, 0, t, :], ALU.subtract).then_inc(rest_ready, 1)
                dve.wait_ge(rest_ready, t + 1)


            def pick(t):
                name = f"logits{t}"
                dve.wait_ge(psum_full, full(name))
                v.scalar_tensor_tensor(out=logits[:, t, :], in0=bank(name)[:, 0:EXPERTS],
                                       scalar=inv_root[:, ROOT_COLS[3 + t]], in1=b_rt[:, :],
                                       op0=ALU.mult, op1=ALU.add).then_inc(freed["dve"], 1)
                dve.wait_ge(freed["dve"], drained(name))
                then(v.max(top_v[:, t, :], logits[:, t, :]))
                then(v.max_index(top_i[:, t, :], top_v[:, t, :], logits[:, t, :]))
                shape = [P, TOP_K, EXPERTS]
                then(v.tensor_tensor(onehot[:, t, :, :], expert_ids.rearrange("p (a e) -> p a e", a=1).to_broadcast(shape),
                                     top_i[:, t, 0:TOP_K].rearrange("p (j a) -> p j a", a=1).to_broadcast(shape),
                                     ALU.is_equal))
                v.tensor_reduce(picked[:, t, :], onehot[:, t, :, :].rearrange("p j e -> p e j"), AX.X, ALU.max) \
                    .then_inc(picked_ready, 1)
                v.tensor_scalar(negtop[:, t:t + 1], top_v[:, t, 0:1], -1.0, None, ALU.mult).then_inc(topv_ready, 1)

            dve.wait_ge(gains_in, 32)
            add_mix(0)
            h_roots(0)
            norm_h(0)
            then(v.tensor_copy(u_parts[:, 0, 0, :], u[:, 0, :]))
            dve.wait_ge(pool_done, 2)
            u_less_part0(0)
            add_mix(1)
            pick(0)
            h_roots(1)
            norm_h(1)
            pick(1)
            dve.wait_ge(parts_ready, 2)
            u_less_part0(1)
            dve.wait_ge(picked_ready, TT)
            then(v.tensor_scalar(unpicked[:, :, :], picked[:, :, :], UNPICKED, UNPICKED, ALU.mult, ALU.subtract))
            dve.wait_ge(psum_full, full("pos"))
            pos = bank("pos")
            then(v.tensor_tensor(slot_of[:, :, 0:EXPERTS], pos[:, 0:64].rearrange("p (t e) -> p t e", t=TT),
                                 unpicked[:, :, :], ALU.add))

            def gates_by_expert():
                dve.wait_ge(gexp_ready, TT)
                then(v.reciprocal(gsum[:, :], gsum[:, :]))
                shape = [P, TOP_K, EXPERTS]
                for t in range(TT):
                    then(v.tensor_scalar(gate4[:, t, :], gate4[:, t, :], gsum[:, t:t + 1], None, ALU.mult))
                    then(v.tensor_tensor(gated[:, t, :, :], onehot[:, t, :, :],
                                         gate4[:, t, :].rearrange("p (j a) -> p j a", a=1).to_broadcast(shape), ALU.mult))
                    then(v.tensor_reduce(gates[:, t, :], gated[:, t, :, :].rearrange("p j e -> p e j"), AX.X, ALU.add))

            def select(e):
                for t in range(TT):
                    ins = v.tensor_scalar(sel[:, t, :], slot_ids[:, 0:SLOTS], slot_of[:, t, bass.ds(e, 1)], None, ALU.is_equal)
                ins.then_inc(sel_ready, 1)

            def add_combined(t, at):
                v.tensor_tensor(acc[:, t, :], acc[:, t, :], psum[:, at:at + 2, :].rearrange("p b n -> p (b n)"),
                                ALU.add).then_inc(comb_added, 1)

            def one_round(r):
                g0 = r * (EXPERTS + 1)
                first = isinstance(r, int)
                if not first:
                    v.tensor_scalar(slot_of[:, :, :], slot_of[:, :, :], float(SLOTS), None, ALU.subtract).then_inc(moved, 1)
                    dve.wait_ge(moved, r)
                    select(0)
                v.memset(cab[:, :, :], 0.0).then_inc(cab_ready, 1)
                with dve.Fori(0, EXPERTS) as e:
                    i = r * EXPERTS + e
                    g = r * (EXPERTS + 1) + e
                    dve.wait_ge(gath_done, g + 1)
                    select(e + 1)
                    dve.wait_ge(cT_done, i + 1)
                    for t in range(TT):
                        ins = v.tensor_scalar(gs[:, t, :], slot_ids, slot_of[:, t, bass.ds(e, 1)],
                                              gates[:, t, bass.ds(e, 1)], ALU.is_equal, ALU.mult)
                    ins.then_inc(gs_ready, 1)
                    dve.wait_ge(rows_used, i + 1)
                    v.tensor_scalar(sel_row[:, :], ones[0:3 * EXPERTS, 0:SLOTS], piece_row[0:3 * EXPERTS, bass.ds(e, 1)],
                                    None, ALU.mult).then_inc(row_ready, 1)
                    dve.wait_ge(comb_done, 2 * g + 1)
                    add_combined(0, CB)
                    dve.wait_ge(h_ready[0], i + 1)
                    v.tensor_scalar(gm, psum[:, H0, :], LIMIT, None, ALU.min).then_inc(gm_ready, 1)
                    dve.wait_ge(h_ready[1], i + 2)
                    v.tensor_scalar(lc, psum[:, H1, :], LIMIT, -LIMIT, ALU.min, ALU.max).then_inc(lc_ready, 1)
                    dve.wait_ge(lc_ready, i + 2)
                    v.scalar_tensor_tensor(out=lg, in0=lc, scalar=1.0, in1=gm, op0=ALU.add, op1=ALU.mult) \
                        .then_inc(lg_ready, 1)
                    dve.wait_ge(lg_ready, i + 1)
                    dve.wait_ge(sg_ready, i + 1)
                    v.tensor_tensor(act, lg, sg, ALU.mult).then_inc(a_ready, 1)
                    dve.wait_ge(comb_done, 2 * g + 2)
                    add_combined(1, CB)
                for t in range(TT):
                    dve.wait_ge(comb_done, 2 * (g0 + EXPERTS) + t + 1)
                    add_combined(t, (CB, H0)[t])
                cols = ROOT_COLS[5]
                w, root, t_ = root_of[:, cols], inv_root[:, cols], root_t[:, cols]
                dve.wait_ge(comb_added, 2 * (g0 + EXPERTS) + 3)
                v.tensor_tensor_reduce(result[:, 1, :], acc[:, 1, :], acc[:, 1, :], 1.0, 0.0,
                                       ALU.mult, ALU.add, ss[:, 1:2]).then_inc(final_step, 1)
                dve.wait_ge(final_step, 6 * r + 1)
                dve.wait_ge(final_sq, r + 1)
                v.tensor_scalar(w, ss[:, 0:TT], 1.0 / DM, RMS_EPS, ALU.mult, ALU.add).then_inc(final_w, 1)
                dve.wait_ge(final_seed, r + 1)
                v.reciprocal(root, root_sqrt[:, cols]).then_inc(final_step, 1)
                dve.wait_ge(final_step, 6 * r + 2)
                v.tensor_tensor(t_, root, root, ALU.mult).then_inc(final_step, 1)
                dve.wait_ge(final_step, 6 * r + 3)
                v.tensor_tensor(t_, t_, w, ALU.mult).then_inc(final_step, 1)
                dve.wait_ge(final_step, 6 * r + 4)
                v.tensor_scalar(t_, t_, -0.5, 1.5, ALU.mult, ALU.add).then_inc(final_step, 1)
                dve.wait_ge(final_step, 6 * r + 5)
                v.tensor_tensor(root, root, t_, ALU.mult).then_inc(final_step, 1)
                dve.wait_ge(final_step, 6 * r + 6)
                for t, part in RESULT_PARTS:
                    col = cols.start + t
                    v.scalar_tensor_tensor(out=result[:, t, part], in0=acc[:, t, part], scalar=inv_root[:, col:col + 1],
                                           in1=area("g_final")[:, part], op0=ALU.mult, op1=ALU.mult) \
                        .then_inc(final_ready, 1)

            select(0)
            v.tensor_reduce(most[0:1, 0:1], pos[0:1, 64:96], AX.X, ALU.max).then_inc(routed, 1)
            dve.wait_ge(parts_ready, 3)
            v.tensor_tensor(u_parts[:, 2, 1, :], u_rest[:, 1, :], u_parts[:, 1, 1, :], ALU.subtract).then_inc(split_done, 1)
            gates_by_expert()
            dve.wait_ge(rows_ready, 1)
            rounds(dve, one_round)


DVE_ROTATED = 17

_INS = ["x", "norm_mix_g", "w_in", "b_forget", "w_out", "norm_ffn_g", "w_router", "b_router",
        "w_exp_in", "b_exp_in", "w_exp_out", "b_exp_out", "norm_final_g"]


def kernel(**inputs):
    import numpy as _np
    import concourse.bacc as _bacc
    from concourse import mybir as _mybir
    from concourse.bass_utils import run_bass_kernel_spmd as _run

    nc = _bacc.Bacc("TRN2", target_bir_lowering=False, num_devices=1)
    arrays, args = {}, []
    given = [(name, _np.ascontiguousarray(inputs[name])) for name in _INS] + [("table", constant_table())]
    for name, a in given:
        arrays[f"in_{name}"] = a
        args.append(nc.dram_tensor(f"in_{name}", a.shape, _mybir.dt.from_np(a.dtype), kind="ExternalInput").ap())
    o = nc.dram_tensor("out_0", (1, SEQ, DM), _mybir.dt.float32, kind="ExternalOutput").ap()
    build(nc, *args, o)
    r = _run(nc, [arrays], core_ids=[0])
    return r.results[0]["out_0"]
```
